# Optimizing a Trainium2 kernel written in Bass

```python
import math
import jax, jax.numpy as jnp
from jax import lax
import numpy as np

D_MODEL = 1024
BATCH = 1
SEQ = 256
DEPTH = 2

HEAD_DIM = 64
N_BRANCH = 4
BRANCH_WIDTH = D_MODEL // N_BRANCH
POOL_WINDOWS = (2, 4, 8, 16)
N_POOL_GROUPS = len(POOL_WINDOWS)
POOL_GROUP = BRANCH_WIDTH // N_POOL_GROUPS
CONV_K = 3
MOBA_HEADS = BRANCH_WIDTH // HEAD_DIM
MOBA_BLOCK = 256
MOBA_TOPK = 3
MOBA_Q_CHUNK = 64
FOX_HEADS = BRANCH_WIDTH // HEAD_DIM
FOX_Q_BLOCK = 128
D_FF = 4 * D_MODEL
ROPE_THETA = 500000.0
ROPE_DIM = HEAD_DIM // 4
ALPHA = (2 * DEPTH) ** 0.25
BETA = (8 * DEPTH) ** -0.25
LN_EPS = 1e-5
FORGET_BIAS_INIT = 2.0
IN_SPLIT_WIDTHS = (BRANCH_WIDTH,) * 10 + (FOX_HEADS, N_BRANCH * D_MODEL)
IN_WIDTH = 10 * BRANCH_WIDTH + FOX_HEADS + N_BRANCH * D_MODEL
FORGET_COL0 = 10 * BRANCH_WIDTH


def _in_split_points():
    pts, acc = [], 0
    for w in IN_SPLIT_WIDTHS[:-1]:
        acc += w
        pts.append(acc)
    return pts

def layer_norm(x):
    xf = x.astype(jnp.float32)
    mu = jnp.mean(xf, axis=-1, keepdims=True)
    var = jnp.mean(jnp.square(xf - mu), axis=-1, keepdims=True)
    return ((xf - mu) * lax.rsqrt(var + LN_EPS)).astype(x.dtype)

def rotary_tables(positions):
    inv = ROPE_THETA ** (-jnp.arange(0, ROPE_DIM, 2, dtype=jnp.float32) / ROPE_DIM)
    ang = positions.astype(jnp.float32)[..., None] * inv
    return jnp.cos(ang)[:, None], jnp.sin(ang)[:, None]

def apply_partial_rotary(t, cos, sin):
    half = ROPE_DIM // 2
    t1, t2, rest = t[..., :half], t[..., half:ROPE_DIM], t[..., ROPE_DIM:]
    r1 = (t1 * cos - t2 * sin).astype(t.dtype)
    r2 = (t2 * cos + t1 * sin).astype(t.dtype)
    return jnp.concatenate([r1, r2, rest], axis=-1)

def to_heads(t, n_heads):
    b, s, _ = t.shape
    return t.reshape(b, s, n_heads, HEAD_DIM).transpose(0, 2, 1, 3)

def from_heads(t):
    b, h, s, d = t.shape
    return t.transpose(0, 2, 1, 3).reshape(b, s, h * d)

def pool_mixer(p, w_pool, pool_scale):
    s = p.shape[1]
    t = jnp.arange(s)
    groups = jnp.split(p, N_POOL_GROUPS, axis=-1)
    outs = []
    for g, w in zip(groups, POOL_WINDOWS):
        cs = jnp.cumsum(g.astype(jnp.float32), axis=1)
        cs_prev = jnp.pad(cs, ((0, 0), (w, 0), (0, 0)))[:, :s]
        cnt = jnp.minimum(t + 1, w).astype(jnp.float32)[None, :, None]
        outs.append(((cs - cs_prev) / cnt).astype(p.dtype) - g)
    pooled = jnp.stack(outs, axis=2)
    mixed = jnp.einsum('bsgc,gcd->bsgd', pooled, w_pool)
    return mixed.reshape(p.shape) * pool_scale

def short_conv_mixer(gate_b, gate_c, h, conv_w):
    v = gate_c * h
    z = lax.conv_general_dilated(
        v, conv_w[:, None, :], window_strides=(1,), padding=[(CONV_K - 1, 0)],
        dimension_numbers=('NWC', 'WIO', 'NWC'), feature_group_count=v.shape[-1])
    return gate_b * z

def moba_attention(q, k, v):
    b, h, s, hd = q.shape
    nblk = -(-s // MOBA_BLOCK)
    s_pad = nblk * MOBA_BLOCK
    pad = ((0, 0), (0, 0), (0, s_pad - s), (0, 0))
    kb = jnp.pad(k, pad).reshape(b, h, nblk, MOBA_BLOCK, hd)
    vb = jnp.pad(v, pad).reshape(b, h, nblk, MOBA_BLOCK, hd)
    kbar = jnp.mean(kb.astype(jnp.float32), axis=3)
    n_sel = min(MOBA_TOPK, nblk)
    scale = HEAD_DIM ** -0.5
    bi = jnp.arange(b)[:, None, None, None]
    hi = jnp.arange(h)[None, :, None, None]
    blk_ids = jnp.arange(nblk)
    n_chunks = s // MOBA_Q_CHUNK

    def chunk(ci):
        t0 = ci * MOBA_Q_CHUNK
        qc = lax.dynamic_slice_in_dim(q, t0, MOBA_Q_CHUNK, axis=2)
        tq = t0 + jnp.arange(MOBA_Q_CHUNK)
        own = t0 // MOBA_BLOCK
        score = jnp.einsum('bhqd,bhnd->bhqn', qc.astype(jnp.float32), kbar)
        score = jnp.where(blk_ids < own, score, -jnp.inf)
        _, idx = lax.top_k(score, n_sel)
        sel_valid = idx < own
        k_sel = kb[bi, hi, idx]
        v_sel = vb[bi, hi, idx]
        l_sel = jnp.einsum('bhqd,bhqkld->bhqkl', qc, k_sel).astype(jnp.float32) * scale
        l_sel = jnp.where(sel_valid[..., None], l_sel, -jnp.inf)
        k_own = lax.dynamic_index_in_dim(kb, own, axis=2, keepdims=False)
        v_own = lax.dynamic_index_in_dim(vb, own, axis=2, keepdims=False)
        l_own = jnp.einsum('bhqd,bhld->bhql', qc, k_own).astype(jnp.float32) * scale
        pos_own = own * MOBA_BLOCK + jnp.arange(MOBA_BLOCK)
        l_own = jnp.where(pos_own[None, :] <= tq[:, None], l_own, -jnp.inf)
        n_k = n_sel * MOBA_BLOCK
        logits = jnp.concatenate([l_sel.reshape(b, h, MOBA_Q_CHUNK, n_k), l_own], axis=-1)
        p = jax.nn.softmax(logits, axis=-1)
        p_sel = p[..., :n_k].reshape(b, h, MOBA_Q_CHUNK, n_sel, MOBA_BLOCK).astype(v.dtype)
        p_own = p[..., n_k:].astype(v.dtype)
        return (jnp.einsum('bhqkl,bhqkld->bhqd', p_sel, v_sel)
                + jnp.einsum('bhql,bhld->bhqd', p_own, v_own))

    out = lax.map(chunk, jnp.arange(n_chunks))
    return out.transpose(1, 2, 0, 3, 4).reshape(b, h, s, hd)

def forgetting_attention(q, k, v, log_f):
    b, h, s, hd = q.shape
    cum = jnp.cumsum(log_f, axis=-1)
    scale = HEAD_DIM ** -0.5
    s_pos = jnp.arange(s)

    def block(qi):
        t0 = qi * FOX_Q_BLOCK
        qb = lax.dynamic_slice_in_dim(q, t0, FOX_Q_BLOCK, axis=2)
        cq = lax.dynamic_slice_in_dim(cum, t0, FOX_Q_BLOCK, axis=2)
        tq = t0 + jnp.arange(FOX_Q_BLOCK)
        logits = (jnp.einsum('bhqd,bhkd->bhqk', qb, k).astype(jnp.float32) * scale
                  + cq[..., :, None] - cum[..., None, :])
        logits = jnp.where(s_pos[None, :] <= tq[:, None], logits, -jnp.inf)
        p = jax.nn.softmax(logits, axis=-1)
        return jnp.einsum('bhqk,bhkd->bhqd', p.astype(v.dtype), v)

    out = lax.map(block, jnp.arange(s // FOX_Q_BLOCK))
    return out.transpose(1, 2, 0, 3, 4).reshape(b, h, s, hd)

def hybrid_layer(x, cond_act, cos, sin, w_ada, b_ada, w_in, b_in, w_pool, pool_scale, conv_w,
                 w_branch, w_o, ln1_g, ln1_b, w_up, b_up, w_down, ln2_g, ln2_b):
    ada = (cond_act @ w_ada + b_ada)[:, None, :]
    sh1, sc1, g1, sh2, sc2, g2 = jnp.split(ada, 6, axis=-1)

    u = layer_norm(x) * (1 + sc1) + sh1
    proj = u @ w_in + b_in
    (p_in, c_b, c_c, c_h, mq, mk, mv, fq, fk, fv, f_logit, gate_logit) = jnp.split(
        proj, _in_split_points(), axis=-1)

    y_pool = pool_mixer(p_in, w_pool, pool_scale)
    y_conv = short_conv_mixer(c_b, c_c, c_h, conv_w)
    q_m = apply_partial_rotary(to_heads(mq, MOBA_HEADS), cos, sin)
    k_m = apply_partial_rotary(to_heads(mk, MOBA_HEADS), cos, sin)
    y_moba = from_heads(moba_attention(q_m, k_m, to_heads(mv, MOBA_HEADS)))
    log_f = jax.nn.log_sigmoid(f_logit.astype(jnp.float32)).transpose(0, 2, 1)
    y_fox = from_heads(forgetting_attention(to_heads(fq, FOX_HEADS), to_heads(fk, FOX_HEADS),
                                            to_heads(fv, FOX_HEADS), log_f))

    gates = jax.nn.sigmoid(gate_logit)
    branches = (y_pool, y_conv, y_moba, y_fox)
    merged = None
    for n in range(N_BRANCH):
        term = gates[..., n * D_MODEL:(n + 1) * D_MODEL] * (branches[n] @ w_branch[n])
        merged = term if merged is None else merged + term
    mixed = merged @ w_o
    x = layer_norm(ALPHA * x + g1 * mixed) * ln1_g + ln1_b

    u2 = layer_norm(x) * (1 + sc2) + sh2
    hdn = jnp.square(jax.nn.relu(u2 @ w_up + b_up))
    x = layer_norm(ALPHA * x + g2 * (hdn @ w_down)) * ln2_g + ln2_b
    return x

def first_inputs(seed: int = 0) -> dict:
    key = jax.random.key(seed)
    ks = jax.random.split(key, 24)
    f32 = jnp.float32
    nrm = lambda k, shape, s: jax.random.normal(k, shape, f32) * s
    x = jax.random.normal(ks[0], (BATCH, SEQ, D_MODEL), f32)
    c = jax.random.normal(ks[1], (BATCH, D_MODEL), f32)
    offsets = jax.random.randint(ks[2], (BATCH, 1), 0, 1024, dtype=jnp.int32)
    positions = jnp.arange(SEQ, dtype=jnp.int32)[None, :] + offsets
    w_ada = nrm(ks[3], (DEPTH, D_MODEL, 6 * D_MODEL), D_MODEL ** -0.5)
    b_ada = nrm(ks[4], (DEPTH, 6 * D_MODEL), 0.01)
    w_in = nrm(ks[5], (DEPTH, D_MODEL, IN_WIDTH), D_MODEL ** -0.5)
    b_in_raw = nrm(ks[6], (DEPTH, IN_WIDTH), 0.01)
    forget_b = FORGET_BIAS_INIT + nrm(ks[7], (DEPTH, FOX_HEADS), 0.1)
    b_in = jnp.concatenate([b_in_raw[:, :FORGET_COL0], forget_b,
                            b_in_raw[:, FORGET_COL0 + FOX_HEADS:]], axis=-1)
    w_pool = nrm(ks[8], (DEPTH, N_POOL_GROUPS, POOL_GROUP, POOL_GROUP), POOL_GROUP ** -0.5)
    pool_scale = 1.0 + nrm(ks[9], (DEPTH, BRANCH_WIDTH), 0.02)
    conv_w = nrm(ks[10], (DEPTH, CONV_K, BRANCH_WIDTH), CONV_K ** -0.5)
    w_branch = nrm(ks[11], (DEPTH, N_BRANCH, BRANCH_WIDTH, D_MODEL), BRANCH_WIDTH ** -0.5)
    w_o = nrm(ks[12], (DEPTH, D_MODEL, D_MODEL), BETA * D_MODEL ** -0.5)
    ln1_g = 1.0 + nrm(ks[13], (DEPTH, D_MODEL), 0.02)
    ln1_b = nrm(ks[14], (DEPTH, D_MODEL), 0.02)
    w_up = nrm(ks[15], (DEPTH, D_MODEL, D_FF), D_MODEL ** -0.5)
    b_up = nrm(ks[16], (DEPTH, D_FF), 0.01)
    w_down = nrm(ks[17], (DEPTH, D_FF, D_MODEL), BETA * D_FF ** -0.5)
    ln2_g = 1.0 + nrm(ks[18], (DEPTH, D_MODEL), 0.02)
    ln2_b = nrm(ks[19], (DEPTH, D_MODEL), 0.02)
    return {"x": x, "c": c, "positions": positions, "w_ada": w_ada, "b_ada": b_ada,
            "w_in": w_in, "b_in": b_in, "w_pool": w_pool, "pool_scale": pool_scale,
            "conv_w": conv_w, "w_branch": w_branch, "w_o": w_o, "ln1_g": ln1_g, "ln1_b": ln1_b,
            "w_up": w_up, "b_up": b_up, "w_down": w_down, "ln2_g": ln2_g, "ln2_b": ln2_b}

def first_block(x, c, positions, w_ada, b_ada, w_in, b_in, w_pool, pool_scale, conv_w, w_branch,
              w_o, ln1_g, ln1_b, w_up, b_up, w_down, ln2_g, ln2_b):
    cos, sin = rotary_tables(positions)
    cond_act = jax.nn.silu(c)
    for l in range(DEPTH):
        x = hybrid_layer(x, cond_act, cos, sin, w_ada[l], b_ada[l], w_in[l], b_in[l], w_pool[l],
                         pool_scale[l], conv_w[l], w_branch[l], w_o[l], ln1_g[l], ln1_b[l],
                         w_up[l], b_up[l], w_down[l], ln2_g[l], ln2_b[l])
    return x


RET_HEADS = 4
RET_DK = 256
RET_DV = 512
RET_CHUNK = 128
ROPE_BASE = 10000.0
GN_EPS = 1e-5
NSA_HEADS = 16
NSA_KV_GROUPS = 2
NSA_HD = 64
CMP_LEN = 32
CMP_STRIDE = 16
CMP_HIDDEN = 256
SEL_BLOCK = 64
SEL_TOPK = 8
WINDOW = 512
NSA_Q_BLOCK = 64
FORCED_SCORE = 1e4
REL_BUCKETS = 32
REL_MAX_DIST = 128
FFN_HIDDEN = -(-8 * D_MODEL // (3 * 256)) * 256
EPS = 1e-6
NEG_INF = -1e30
SPLIT_SIZES = (RET_HEADS * RET_DK, RET_HEADS * RET_DK, RET_HEADS * RET_DV, RET_HEADS * RET_DV,
               NSA_HEADS * NSA_HD, 6 * NSA_KV_GROUPS * NSA_HD, 3 * NSA_HEADS, D_MODEL, D_MODEL)
C_IN = sum(SPLIT_SIZES)


def rms_norm(x, g):
    xf = x.astype(jnp.float32)
    y = xf * lax.rsqrt(jnp.mean(xf * xf, -1, keepdims=True) + EPS)
    return (y * g.astype(jnp.float32)).astype(x.dtype)

def masked_softmax(logits, mask):
    z = jnp.where(mask, logits.astype(jnp.float32), NEG_INF)
    z = z - jnp.max(z, -1, keepdims=True)
    e = jnp.exp(z) * mask
    return e / jnp.maximum(jnp.sum(e, -1, keepdims=True), 1e-30)

def t5_bucket(dist):
    dist = jnp.maximum(dist, 0)
    max_exact = REL_BUCKETS // 2
    large = max_exact + (jnp.log(jnp.maximum(dist, 1).astype(jnp.float32) / max_exact)
                         / math.log(REL_MAX_DIST / max_exact) * (REL_BUCKETS - max_exact)).astype(jnp.int32)
    large = jnp.minimum(large, REL_BUCKETS - 1)
    return jnp.where(dist < max_exact, dist, large)

def rotary(x, pos):
    half = x.shape[-1] // 2
    freqs = ROPE_BASE ** (-jnp.arange(half, dtype=jnp.float32) / half)
    ang = pos.astype(jnp.float32)[:, None] * freqs
    cos = jnp.cos(ang)[None, :, None, :]
    sin = jnp.sin(ang)[None, :, None, :]
    x1, x2 = x[..., :half], x[..., half:]
    return jnp.concatenate([x1 * cos - x2 * sin, x1 * sin + x2 * cos], -1)

def retention(q, k, v):
    B, T, H, dk = q.shape
    dv = v.shape[-1]
    nc = T // RET_CHUNK
    lg = jnp.log(1.0 - 2.0 ** (-5.0 - jnp.arange(H, dtype=jnp.float32)))
    n = jnp.arange(RET_CHUNK, dtype=jnp.float32)
    diff = n[:, None] - n[None, :]
    dmask = jnp.where(diff >= 0, jnp.exp(jnp.maximum(diff, 0.0)[None] * lg[:, None, None]), 0.0)
    xi = jnp.exp((n + 1.0)[None] * lg[:, None])
    zeta = jnp.exp((RET_CHUNK - 1.0 - n)[None] * lg[:, None])
    g_chunk = jnp.exp(RET_CHUNK * lg)

    def to_chunks(t):
        return t.reshape(B, nc, RET_CHUNK, H, t.shape[-1]).transpose(1, 0, 3, 2, 4)

    def step(R, qkv):
        qc, kc, vc = qkv
        s = jnp.einsum('bhnd,bhmd->bhnm', qc, kc) * dmask
        o = (jnp.einsum('bhnm,bhme->bhne', s, vc)
             + jnp.einsum('bhnd,bhde->bhne', qc, R) * xi[:, :, None])
        R = g_chunk[:, None, None] * R + jnp.einsum('bhmd,bhme->bhde', kc * zeta[:, :, None], vc)
        return R, o

    R0 = jnp.zeros((B, H, dk, dv), jnp.float32)
    _, o = lax.scan(step, R0, (to_chunks(q), to_chunks(k), to_chunks(v)))
    return o.transpose(1, 0, 3, 2, 4).reshape(B, T, H, dv)

def compress(kv, pos_emb, w1, w2):
    T = kv.shape[2]
    n_cmp = (T - CMP_LEN) // CMP_STRIDE + 1
    idx = jnp.arange(n_cmp)[:, None] * CMP_STRIDE + jnp.arange(CMP_LEN)[None]
    blocks = kv[:, :, idx, :] + pos_emb
    flat = blocks.reshape(blocks.shape[0], blocks.shape[1], n_cmp, CMP_LEN * NSA_HD)
    return jax.nn.gelu(flat @ w1) @ w2

def nsa(q, k_c, v_c, k_s, v_s, k_w, v_w, gates, pos_k, pos_v, w1_k, w2_k, w1_v, w2_v, rel_bias):
    B, T, H, hd = q.shape
    G = NSA_KV_GROUPS
    HG = H // G
    QB = NSA_Q_BLOCK
    scale = hd ** -0.5
    grp = lambda t: t.transpose(0, 2, 1, 3)
    kc = compress(grp(k_c), pos_k, w1_k, w2_k)
    vc = compress(grp(v_c), pos_v, w1_v, w2_v)
    n_cmp = kc.shape[2]
    cmp_end = jnp.arange(n_cmp) * CMP_STRIDE + CMP_LEN - 1
    n_sel = T // SEL_BLOCK
    sel_k = min(SEL_TOPK, n_sel)
    sel_start = jnp.arange(n_sel) * SEL_BLOCK
    overlap = ((cmp_end[:, None] - CMP_LEN + 1 < sel_start[None] + SEL_BLOCK)
               & (cmp_end[:, None] >= sel_start[None])).astype(jnp.float32)
    ks_blocks = grp(k_s).reshape(B, G, n_sel, SEL_BLOCK, hd)
    vs_blocks = grp(v_s).reshape(B, G, n_sel, SEL_BLOCK, hd)
    kw_pad = jnp.pad(grp(k_w), ((0, 0), (0, 0), (WINDOW, 0), (0, 0)))
    vw_pad = jnp.pad(grp(v_w), ((0, 0), (0, 0), (WINDOW, 0), (0, 0)))
    table = rel_bias.reshape(REL_BUCKETS, G, HG).astype(jnp.float32)
    nq = T // QB
    qb = q.reshape(B, nq, QB, G, HG, hd).transpose(1, 0, 3, 4, 2, 5)
    gb = gates.reshape(B, nq, QB, G, HG, 3).transpose(1, 0, 3, 4, 2, 5)
    starts = jnp.arange(nq, dtype=jnp.int32) * QB
    bidx = jnp.arange(B)[:, None, None, None]
    gidx = jnp.arange(G)[None, :, None, None]
    jj = jnp.arange(n_sel)

    def head_bias(dist):
        return jnp.moveaxis(table[t5_bucket(dist)], (-2, -1), (0, 1))

    def sel_bias(dist):
        b = jax.vmap(lambda tb, bk: tb[bk], in_axes=(1, 1), out_axes=1)(table, t5_bucket(dist))
        return jnp.moveaxis(b, -1, 2)

    def block(args):
        qx, gx, s = args
        pos = s + jnp.arange(QB, dtype=jnp.int32)
        dc = pos[:, None] - cmp_end[None]
        lc = jnp.einsum('bghqd,bgnd->bghqn', qx, kc) * scale + head_bias(dc)
        pc = masked_softmax(lc, dc >= 0)
        oc = jnp.einsum('bghqn,bgnd->bghqd', pc.astype(vc.dtype), vc)
        imp = jnp.einsum('bghqn,nj->bgqj', pc, overlap)
        cur = pos // SEL_BLOCK
        forced = (jj[None] == 0) | (jj[None] == cur[:, None]) | (jj[None] == cur[:, None] - 1)
        imp = jnp.where(forced, FORCED_SCORE, imp)
        imp = jnp.where(sel_start[None] <= pos[:, None], imp, NEG_INF)
        _, sel = lax.top_k(imp, sel_k)
        ksel = ks_blocks[bidx, gidx, sel]
        vsel = vs_blocks[bidx, gidx, sel]
        kpos = sel[..., None] * SEL_BLOCK + jnp.arange(SEL_BLOCK)
        ds = pos[:, None, None] - kpos
        ls = jnp.einsum('bghqd,bgqkld->bghqkl', qx, ksel) * scale + sel_bias(ds)
        bsz, g_, hg_, qn, kk, bs = ls.shape
        ps = masked_softmax(ls.reshape(bsz, g_, hg_, qn, kk * bs),
                            (ds >= 0)[:, :, None].reshape(bsz, g_, 1, qn, kk * bs))
        os_ = jnp.einsum('bghqm,bgqmd->bghqd', ps.astype(vsel.dtype),
                         vsel.reshape(bsz, g_, qn, kk * bs, hd))
        kw = lax.dynamic_slice_in_dim(kw_pad, s, WINDOW + QB, axis=2)
        vw = lax.dynamic_slice_in_dim(vw_pad, s, WINDOW + QB, axis=2)
        wpos = s - WINDOW + jnp.arange(WINDOW + QB, dtype=jnp.int32)
        dw = pos[:, None] - wpos[None]
        lw = jnp.einsum('bghqd,bgld->bghql', qx, kw) * scale + head_bias(dw)
        pw = masked_softmax(lw, (dw >= 0) & (dw < WINDOW) & (wpos[None] >= 0))
        ow = jnp.einsum('bghql,bgld->bghqd', pw.astype(vw.dtype), vw)
        return gx[..., 0:1] * oc + gx[..., 1:2] * os_ + gx[..., 2:3] * ow

    out = lax.map(block, (qb, gb, starts))
    return out.transpose(1, 0, 4, 2, 3, 5).reshape(B, T, H * hd)

def second_inputs(seed: int = 0) -> dict:
    key = jax.random.key(seed)
    ks = jax.random.split(key, 20)
    nrm = lambda k, shape, fan: jax.random.normal(k, shape, jnp.float32) * (fan ** -0.5)
    gain = lambda k, shape: 1.0 + 0.01 * jax.random.normal(k, shape, jnp.float32)
    L = DEPTH
    return {
        "x": jax.random.normal(ks[0], (BATCH, SEQ, D_MODEL), jnp.float32),
        "norm_mix_g": gain(ks[1], (L, D_MODEL)),
        "w_in": nrm(ks[2], (L, D_MODEL, C_IN), D_MODEL),
        "cmp_pos_k": 0.02 * jax.random.normal(ks[3], (L, CMP_LEN, NSA_HD), jnp.float32),
        "cmp_pos_v": 0.02 * jax.random.normal(ks[4], (L, CMP_LEN, NSA_HD), jnp.float32),
        "cmp_w1_k": nrm(ks[5], (L, CMP_LEN * NSA_HD, CMP_HIDDEN), CMP_LEN * NSA_HD),
        "cmp_w2_k": nrm(ks[6], (L, CMP_HIDDEN, NSA_HD), CMP_HIDDEN),
        "cmp_w1_v": nrm(ks[7], (L, CMP_LEN * NSA_HD, CMP_HIDDEN), CMP_LEN * NSA_HD),
        "cmp_w2_v": nrm(ks[8], (L, CMP_HIDDEN, NSA_HD), CMP_HIDDEN),
        "w_o_ret": nrm(ks[9], (L, RET_HEADS * RET_DV, D_MODEL), RET_HEADS * RET_DV),
        "w_o_nsa": nrm(ks[10], (L, NSA_HEADS * NSA_HD, D_MODEL), NSA_HEADS * NSA_HD),
        "w_out": nrm(ks[11], (L, D_MODEL, D_MODEL), D_MODEL),
        "norm_ffn_g": gain(ks[12], (L, D_MODEL)),
        "w_ffn_in": nrm(ks[13], (L, D_MODEL, 2 * FFN_HIDDEN), D_MODEL),
        "w_ffn_out": nrm(ks[14], (L, FFN_HIDDEN, D_MODEL), FFN_HIDDEN),
        "rel_bias": 0.2 * jax.random.normal(ks[15], (REL_BUCKETS, NSA_HEADS), jnp.float32),
        "norm_final_g": gain(ks[16], (D_MODEL,)),
    }

def second_block(x, norm_mix_g, w_in, cmp_pos_k, cmp_pos_v, cmp_w1_k, cmp_w2_k, cmp_w1_v, cmp_w2_v,
              w_o_ret, w_o_nsa, w_out, norm_ffn_g, w_ffn_in, w_ffn_out, rel_bias, norm_final_g):
    B, T, _ = x.shape
    pos = jnp.arange(T, dtype=jnp.int32)
    cuts = [int(c) for c in np.cumsum(SPLIT_SIZES)[:-1]]
    for i in range(DEPTH):
        h = rms_norm(x, norm_mix_g[i])
        proj = h @ w_in[i]
        q_r, k_r, v_r, g_r, q_n, kv_n, gate_n, m_a, m_b = jnp.split(proj, cuts, axis=-1)
        qr = rotary(q_r.reshape(B, T, RET_HEADS, RET_DK).astype(jnp.float32), pos)
        kr = rotary(k_r.reshape(B, T, RET_HEADS, RET_DK).astype(jnp.float32), pos) * (RET_DK ** -0.5)
        vr = v_r.reshape(B, T, RET_HEADS, RET_DV).astype(jnp.float32)
        o_r = retention(qr, kr, vr)
        mu = jnp.mean(o_r, -1, keepdims=True)
        var = jnp.mean(jnp.square(o_r - mu), -1, keepdims=True)
        o_r = ((o_r - mu) * lax.rsqrt(var + GN_EPS)).reshape(B, T, RET_HEADS * RET_DV).astype(x.dtype)
        y_ret = (jax.nn.silu(g_r) * o_r) @ w_o_ret[i]
        kv = kv_n.reshape(B, T, 6, NSA_KV_GROUPS, NSA_HD)
        o_n = nsa(q_n.reshape(B, T, NSA_HEADS, NSA_HD),
                  kv[:, :, 0], kv[:, :, 1], kv[:, :, 2], kv[:, :, 3], kv[:, :, 4], kv[:, :, 5],
                  jax.nn.sigmoid(gate_n).reshape(B, T, NSA_HEADS, 3),
                  cmp_pos_k[i], cmp_pos_v[i], cmp_w1_k[i], cmp_w2_k[i], cmp_w1_v[i], cmp_w2_v[i],
                  rel_bias)
        y_nsa = o_n.astype(x.dtype) @ w_o_nsa[i]
        mixed = (jax.nn.sigmoid(m_a) * y_ret + jax.nn.sigmoid(m_b) * y_nsa) @ w_out[i]
        x = x + mixed.astype(x.dtype)
        h = rms_norm(x, norm_ffn_g[i])
        a, b = jnp.split(h @ w_ffn_in[i], 2, axis=-1)
        x = x + ((jax.nn.silu(a) * b) @ w_ffn_out[i]).astype(x.dtype)
    return rms_norm(x, norm_final_g)


def setup_inputs(seed=0):
    out = dict(first_inputs(seed))
    for name, value in second_inputs(seed + 1).items():
        if name != "x":
            out[name + "_2"] = value
    return out


def reference(
    x, c, positions, w_ada, b_ada, w_in, b_in, w_pool, pool_scale, conv_w, w_branch, w_o, ln1_g,
    ln1_b, w_up, b_up, w_down, ln2_g, ln2_b, norm_mix_g_2, w_in_2, cmp_pos_k_2, cmp_pos_v_2,
    cmp_w1_k_2, cmp_w2_k_2, cmp_w1_v_2, cmp_w2_v_2, w_o_ret_2, w_o_nsa_2, w_out_2, norm_ffn_g_2,
    w_ffn_in_2, w_ffn_out_2, rel_bias_2, norm_final_g_2,
):
    x = first_block(
        x, c, positions, w_ada, b_ada, w_in, b_in, w_pool, pool_scale, conv_w, w_branch, w_o,
        ln1_g, ln1_b, w_up, b_up, w_down, ln2_g, ln2_b,
    )
    return second_block(
        x, norm_mix_g_2, w_in_2, cmp_pos_k_2, cmp_pos_v_2, cmp_w1_k_2, cmp_w2_k_2, cmp_w1_v_2,
        cmp_w2_v_2, w_o_ret_2, w_o_nsa_2, w_out_2, norm_ffn_g_2, w_ffn_in_2, w_ffn_out_2,
        rel_bias_2, norm_final_g_2,
    )


_drawn_inputs = setup_inputs


def setup_inputs(seed=0):
    import zlib

    import numpy as np

    out = dict(_drawn_inputs(seed))
    spreads = {}
    factors = {'pool_scale': 8.0,
     'b_up': 5.887,
     'norm_mix_g_2': 5.122,
     'cmp_pos_k_2': 8.0,
     'cmp_pos_v_2': 8.0,
     'norm_ffn_g_2': 5.249,
     'norm_final_g_2': 5.412}
    for name, (base, spread) in spreads.items():
        noise = np.random.default_rng([zlib.crc32(name.encode()), seed]).standard_normal(out[name].shape)
        drawn = base * np.exp(spread * noise) if base else spread * noise
        out[name] = __import__('jax').numpy.asarray(drawn.astype(out[name].dtype))
    for name, factor in factors.items():
        out[name] = (out[name] * factor).astype(out[name].dtype)
    return out
```

```python
import math
from contextlib import ExitStack

import numpy as np

import concourse.bass as bass
from concourse import mybir

F32 = mybir.dt.float32
F32R = mybir.dt.float32r
I32 = mybir.dt.int32
ALU = mybir.AluOpType
ACT = mybir.ActivationFunctionType
AX = mybir.AxisListType

P = 128
T = 256
D = 1024
KC = D // P
DEPTH = 2
RING = 4
UW = 1024
AHEAD = 2
HD = 64
HEADS1 = 8
BIG = 1e30
ALPHA = (2 * DEPTH) ** 0.25
LN_EPS = 1e-5
GN_EPS = 1e-5
RMS_EPS = 1e-6
POOL_WINDOWS = (2, 4, 8, 16)
POOL_PAD = max(POOL_WINDOWS)
SCORE_SCALE = HD ** -0.5
PI = math.pi
TWO_PI_A = 6.28125
TWO_PI_B = float(np.float32(2 * PI - TWO_PI_A) // 2.0 ** -21 * 2.0 ** -21)
TWO_PI_C = 2 * PI - TWO_PI_A - TWO_PI_B
ROUND_MAGIC = 1.5 * 2.0 ** 23
SAFE_PI = 3.1415925

ADA = 48
ADA_FIRST = 16
N_PROJ = 20
N_GATE = 32
H1_PROJ = 0
H1_GATE = H1_PROJ + N_PROJ
H1_BRANCH = H1_GATE + N_GATE
H1_WO = H1_BRANCH + KC
H1_FFN = H1_WO + KC
H1 = H1_FFN + 64
V1_GATE = N_PROJ
V1_BRANCH = V1_GATE + N_GATE
V1_WO = V1_BRANCH + 2 * KC
V1_FFN = V1_WO + KC
V1 = V1_FFN + 32
R0 = ADA_FIRST
R1 = H1 + ADA

def columns(parts):
    at, out = 0, {}
    for name, width in parts:
        out[name] = (at, at + width)
        at += width
    return out, at


PAR1, NPAR1 = columns([("b_ada", 48), ("b_proj", 16), ("b_gate", 32), ("b_up", 32), ("ln1_g", 8), ("ln1_b", 8),
                       ("ln2_g", 8), ("ln2_b", 8), ("pool_scale", 2), ("conv_w", 6), ("b_v", 512), ("b_f", 4),
                       ("w_f", 32), ("w_pool", 256)])
CON1, NCON1 = columns([("rot", 128), ("inv_freq", 1), ("tri", 512), ("mask", 384), ("inv_cnt", 512)])


NSA_HEADS = 16
NSA_GROUPS = 2
CMP = 15
CMP_STRIDE = 16
CMP_LC = 16
RET_HEADS = 4
RET_DV = 512
N_KV = 6
N_CMP = 8
FFN2 = 22
H2_CMP = N_KV
H2_Q = H2_CMP + N_CMP
H2_QK = H2_Q + KC
H2_V = H2_QK + 16
H2_PAIR = H2_V + 16
H2_MA = H2_PAIR + 32
H2_MB = H2_MA + KC
H2_ONSA = H2_MB + KC
H2_OUT = H2_ONSA + KC
H2_FFN = H2_OUT + KC
H2 = H2_FFN + 3 * FFN2
R2 = H2
V2_GATE, V2_HID = N_KV, N_KV + 1
V2_SHIFT = 2 - N_CMP
V2_FFN = H2_FFN + V2_SHIFT
V2 = V2_FFN + 2 * FFN2
BODY2 = (("a", 0), ("b", 0), ("a", 1), ("b", 1), ("d", 0), ("a", 2), ("b", 2), ("d", 1), ("a", 3), ("b", 3), ("d", 2), ("d", 3))
TAIL2 = (("a", 0), ("b", 0), ("a", 1), ("b", 1), ("d", 0), ("d", 1))
GELU_CUBE = 0.044715
GELU_SCALE = math.sqrt(2 / math.pi)
PAR2, NPAR2 = columns([("g_mix", 8), ("g_ffn", 8), ("w_gate", 384), ("pos", 32), ("w2k", 256), ("w2v", 128)])
CON2, NCON2 = columns([("cos", 256), ("sin", 256), ("decay", 1024), ("cmask", 30), ("blocks", 512), ("rep", 128),
                       ("g_final", 8)])
HOT = 33
HOT_ROW, HOT_CMP = 384, 2 * CMP * P


def raw_of(h):
    if h < H1_GATE + AHEAD:
        return h
    if h < H1_BRANCH + AHEAD:
        return 2 * h + 1 - (H1_GATE + AHEAD)
    if h < H1_FFN + AHEAD:
        return h + N_GATE
    f = h - (H1_FFN + AHEAD)
    return h + N_GATE + (f + 3) // 4


def build_program(nc, stream, x_in, c_in, positions, par1, con1, ident_in, par2, con2, flip_in, hot, rel_bias,
                  fn_dram, out):
    ctx = ExitStack()
    with ctx:
        def sb(name, shape, dt=F32):
            return ctx.enter_context(nc.sbuf_tensor(name, shape, dt))

        def sem(name):
            return ctx.enter_context(nc.semaphore(name))

        def sems(name):
            return [sem(f"{name}{i}") for i in range(RING)]

        raw = sb("raw", [P, RING, UW])
        w_hi = sb("w_hi", [P, RING, UW], F32R)
        w_lo = sb("w_lo", [P, RING, UW], F32R)
        u_hi = sb("u_hi", [P, KC, T], F32R)
        u_lo = sb("u_lo", [P, KC, T], F32R)
        a_hi = sb("a_hi", [P, KC, T], F32R)
        a_lo = sb("a_lo", [P, KC, T], F32R)
        wf_hi = sb("wf_hi", [P, KC, 4], F32R)
        wf_lo = sb("wf_lo", [P, KC, 4], F32R)
        x = sb("x", [P, KC, T])
        y = sb("y", [P, KC, T])
        sd = sb("sd", [P, T])
        rstd = sb("rstd", [P, T])
        ident = sb("ident", [P, P])
        ones_d = sb("ones_d", [P, P])
        zeros = sb("zeros", [P, 2 * T], F32)
        eps = sb("eps", [P, 4])
        par = sb("par", [P, max(NPAR1, NPAR2)])
        arena = sb("arena", [P, 25500])
        used = [0]

        def take(*dims):
            n = int(np.prod(dims))
            v = arena[:, used[0]:used[0] + n]
            used[0] += n
            if len(dims) == 2:
                return v.rearrange("p (a b) -> p a b", b=dims[1])
            if len(dims) == 3:
                return v.rearrange("p (a b c) -> p a b c", b=dims[1], c=dims[2])
            return v

        gates = take(32, T)
        sq = gates[:, 0:KC, :]
        proj = take(8, T)
        qk = take(8, T)
        prod = qk.rearrange("p (a b) t -> p a b t", a=2)
        v_tok = take(2, 512)
        bias = take(HEADS1, 384)
        rot_raw = gates[:, 12:16, :]
        rot_tmp = gates[:, 16:20, :]
        cs = take(2, POOL_PAD + T)
        vv = take(2, 2 + T)
        sneg = take(2, 384)
        pt = take(2, 384)
        q_st = take(T)
        k_st = take(T)
        v_st = take(2, P)
        b_st = take(2, 384)
        tri_b = gates[:, 8:12, :].rearrange("p a (b n) -> p (a b) n", n=P)
        con = take(NCON1)
        cos = take(T)
        sin = take(T)
        ang = gates[:, 20:24, :]
        pos_i = gates[:, 24, :]
        small = take(128)
        c_row = take(D)
        c_tmp = y[:, 0:4, :].rearrange("p a t -> p (a t)")
        msum = proj[:, 0:6, :].rearrange("p (a b) t -> p a b t", a=2)
        ada = sb("ada", [P, ADA])
        ada_t = sb("ada_t", [P, KC])
        mn = sb("mn", [P, 2, 2])
        rs = sb("rs", [P, 2, 2])
        bgh = sb("bgh", [P, 40])
        tmpa = sb("tmpa", [P, 2, T])
        assert used[0] <= 25500

        used[0] = 0
        rq = take(8, T)
        rk = take(8, T)
        rv = take(RET_HEADS, 2, RET_DV)
        sq2 = rq
        sig_b = rq
        yret = take(8, T)
        qn = take(8, T)
        sg = qn
        bias2 = take(NSA_HEADS, T)
        kdup = take(NSA_GROUPS * 2, T)
        vnat = take(2, 2, P)
        sn = take(4, 384)
        pt2 = take(2, 384)
        bc = take(2, NSA_HEADS, CMP)
        q_st2 = take(T)
        b_st2 = take(2, T)
        r4 = take(4, T)
        rt = take(2, T)
        con_2 = take(NCON2)
        gsig = take(2, NSA_HEADS, 3)
        kct = take(30)
        tmp2 = rv.rearrange("p a b c -> p (a b c)")
        hot_sb = tmp2[0:HOT, 0:HOT_CMP]
        hot_row = rk.rearrange("p a b -> p (a b)")[0:HOT, 0:HOT_ROW]
        flip = rk.rearrange("p a b -> p (a b)")[:, 1024:1024 + P]
        table = rk.rearrange("p a b -> p (a b)")[0:HOT, 384:400]
        fn_sb = rk.rearrange("p a b -> p (a b)")[0:NSA_HEADS, 512:512 + HOT_ROW]
        x2 = tmp2[:, 0:960].rearrange("p (k c n) -> p k c n", k=2, c=CMP_LC)
        hx = tmp2[:, 1024:1144]
        gx, gy, gz = (tmp2[0:2 * CMP, 2048 + 512 * j:2560 + 512 * j] for j in range(3))
        x2_hi, x2_lo = (v[:, 2:6, :].rearrange("p a t -> p (a t)")[:, 0:960].rearrange("p (k c n) -> p k c n", k=2, c=CMP_LC)
                        for v in (a_hi, a_lo))
        vcn = tmp2[0:CMP, 1408:1536]
        sc_cmp = tmp2[:, 1536:2016].rearrange("p (t h n) -> p t h n", t=2, h=NSA_HEADS)
        yret_flat = yret.rearrange("p a b -> p (a b)")
        vbd = yret_flat[:, 0:1024].rearrange("p (g h d) -> p g h d", g=2, h=8)
        pc_n = yret_flat[:, 1024:1536].rearrange("p (t h n) -> p t h n", t=2, h=NSA_HEADS)
        pc_t = yret_flat[:, 1536:2048].rearrange("p (g q) -> p g q", g=2)
        assert used[0] <= 25500
        wg_hi = a_hi[:, 0:2, :].rearrange("p a (b n) -> p (a b n)", n=16)[:, 0:384].rearrange("p (c n) -> p c n", n=48)
        wg_lo = a_lo[:, 0:2, :].rearrange("p a (b n) -> p (a b n)", n=16)[:, 0:384].rearrange("p (c n) -> p c n", n=48)
        st_c = sb("st_c", [P, 3, 32])
        w_st = sb("w_st", [P, 2, 2, 2])
        mn2 = sb("mn2", [P, 4, 2])
        rs2 = sb("rs2", [P, 4, 2])
        vm = sb("vm", [P, 2])

        ps = [ctx.enter_context(nc.psum_tensor(f"ps{i}", [P, 512], F32)) for i in range(8)]
        m4, m5, m6, m7 = ps[4:8]

        def pview(bank):
            return bank[:, :].rearrange("p (a t) -> p a t", t=T)

        def pc(name):
            a, b = PAR1[name]
            return par[:, a:b]

        def p2(name):
            a, b = PAR2[name]
            return par[:, a:b]

        def c2(name):
            a, b = CON2[name]
            return con_2[:, a:b]

        def half(h):
            return slice(HD * h, HD * (h + 1))

        def cc(name):
            a, b = CON1[name]
            return con[:, a:b]

        landed, raw_used = sems("landed"), sems("raw_used")
        hi_made, mm_done, psum_used = sems("hi_made"), sems("mm_done"), sems("psum_used")
        names = ("x_in con_in c_in par_in ident_in pos_in setup_dve sin_ready c_tanh consts wf_hi "
                 "wf_ready x_chunk ln_mean ln_cent ln_sq ln_var ln_sd ln_mod ln_scaled x_scaled_out u_hi_made "
                 "u_lo_made x_scaled conv_in rot_in proj_all qkv_ready rot_mm pooled pool_mm y_local f_logit f_abs f_log "
                 "logf_ready cum_ready bias_ready staged scores sneg_ready exp_done probs_ready probs_t "
                 "probs_t_sb pv_done o_hi_made o_stored gates_ready msum_ready m_hi_made merged "
                 "h_hi_made h_ready ffn_done layer_end out_done passed con2_in hot_in table_in tab_ready fn_mm fn_sb fn_out "
                 "bias_in flip_mm flipped bc_mm bc_ready par2_in wg_hi wg_ready x_ready2 x2_raw x2_ready g_tanh gsig_ready kv_ready "
                 "cmp_hid gelu_in gelu_t hid_ready hid_turned hx_ready x2_hi x2_split cmp_w2 cmp_kv vrep vbd_ready q_all cmp_sc cmp_neg cmp_exp cmp_p "
                 "cmp_turn cmp_pt cmp_o cmp_stored staged2 n_scores n_sneg n_exp n_probs n_turn n_pt n_pv o2_stored "
                 "rr_ready rr_done v_ready v_cent r_st r_sts r_ot r_sq r_copy r_var r_sd r_norm g2_tanh sg_ready "
                 "y_ready y_hi y_full ma_all mb_all nsa_hi nsa_full t2_made "
                 "y_last").split()
        S = {n: sem(n) for n in names}

        stream_v = stream
        block = ctx.enter_context(nc.Block())

        def settled(eng):
            eng.sem_inc(S["passed"], 1)

        def at(base, off):
            return off % RING, base + off // RING

        @block.sync
        def _(sp):
            with sp.Fori(0, stream.shape[0]) as n:
                for s in range(RING):
                    sp.wait_ge(raw_used[s], n)
                    sp.dma_start(raw[:, s, :], stream_v[n, s]).then_inc(landed[s], 16)
            for s in range(RING):
                sp.wait_ge(landed[s], 16 * stream.shape[0])
            sp.wait_ge(S["out_done"], 16)

        @block.tensor
        def _(pe):
            def three(out_ap, w, a_h, a_l, hs, first, last):
                pe.matmul(out_ap, w(w_hi, hs), a_h, start=first, stop=False, skip_group_check=True)
                pe.matmul(out_ap, w(w_hi, hs), a_l, start=False, stop=False, skip_group_check=True)
                return pe.matmul(out_ap, w(w_lo, hs), a_h, start=False, stop=last, skip_group_check=True)

            def wait_split(rb, ro):
                rsl, rc = at(rb, ro)
                pe.wait_ge(raw_used[rsl], rc + 1)

            def wait_unit(hb, ho, vb, vo, rb, ro):
                hs, _ = at(hb, ho)
                vs, vc = at(vb, vo)
                wait_split(rb, ro)
                pe.wait_ge(psum_used[vs], vc)
                return hs, vs

            def unit_t(hb, ho, vb, vo, rb, ro, ah, al, before=None):
                hs, vs = wait_unit(hb, ho, vb, vo, rb, ro)
                for k in range(KC):
                    if before:
                        before(k)
                    mm = three(ps[vs][:, 0:T], lambda w, s, k=k: w[:, s, k * P:(k + 1) * P],
                                     ah[:, k, :], al[:, k, :], hs, k == 0, k == KC - 1)
                mm.then_inc(mm_done[hs], 1)

            def pair_n(hb, ho, vb, vo, rb, ro, ah, al):
                hs, _ = at(hb, ho)
                for j in range(2):
                    wait_unit(hb, ho + j, vb, vo + j, rb, ro + j)
                for t in range(2):
                    o = ps[at(vb, vo + t)[0]][:, 0:T].rearrange("p (a n) -> p a n", a=2)
                    for k in range(KC):
                        wh, wl = (w[:, hs:hs + 2, k * P:(k + 1) * P] for w in (w_hi, w_lo))
                        xh, xl = ah[:, k, t * P:(t + 1) * P], al[:, k, t * P:(t + 1) * P]
                        pe.matmul(o, xh, wh, start=k == 0, stop=False)
                        pe.matmul(o, xh, wl, start=False, stop=False)
                        mm = pe.matmul(o, xl, wh, start=False, stop=k == KC - 1)
                mm.then_inc(mm_done[hs], 1)
                pe.drain().then_inc(mm_done[hs + 1], 1)

            def mean(n, ready):
                for c in range(KC):
                    ready(c)
                    mm = pe.matmul(m4[:, 0:T], ones_d[:, :], x[:, c, :], start=c == 0, stop=c == KC - 1)
                mm.then_inc(S["ln_mean"], 1)

            def variance(n, sq=sq):
                for c in range(KC):
                    if c % 2 == 0:
                        pe.wait_ge(S["ln_sq"], 4 * n + c // 2 + 1)
                    mm = pe.matmul(m5[:, 0:T], ones_d[:, :], sq[:, c, :], start=c == 0, stop=c == KC - 1)
                mm.then_inc(S["ln_var"], 1)

            pe.wait_ge(S["consts"], 1)
            pe.wait_ge(S["ident_in"], 16)
            with pe.Fori(0, DEPTH) as l:
                hb, vb, rb = l * (H1 // 4), l * (V1 // 4), R0 // 4 + l * (R1 // 4)
                mean(4 * l, lambda c: pe.wait_ge(S["x_chunk"], 24 * l + c + 1))
                variance(4 * l)
                for k in range(16):
                    ready = (lambda c: pe.wait_ge(S["u_lo_made"], 8 * l + c // 2 + 1)) if k == 0 else None
                    unit_t(hb, k, vb, k, rb, raw_of(k), u_hi, u_lo, ready)
                    if k == 1:
                        pe.wait_ge(S["wf_ready"], l + 1)
                        for t in range(2):
                            o = m6[:, 4 * t:4 * t + 4]
                            for kc in range(KC):
                                uh, ul = u_hi[:, kc, t * P:(t + 1) * P], u_lo[:, kc, t * P:(t + 1) * P]
                                pe.matmul(o, uh, wf_hi[:, kc, :], start=kc == 0, stop=False)
                                pe.matmul(o, uh, wf_lo[:, kc, :], start=False, stop=False)
                                mm = pe.matmul(o, ul, wf_hi[:, kc, :], start=False, stop=kc == KC - 1)
                        mm.then_inc(S["f_logit"], 1)
                    if k == 5:
                        pe.wait_ge(S["logf_ready"], l + 1)
                        tri = cc("tri").rearrange("p (a t) -> p a t", a=2)
                        for t in range(2):
                            for kt in range(2):
                                pe.matmul(m6[:, 16 + 4 * t:20 + 4 * t], tri[:, kt, t * P:(t + 1) * P],
                                          small[:, 16 + 4 * kt:20 + 4 * kt], start=kt == 0, stop=kt == 1)
                        for h in range(4):
                            for kt in range(2):
                                mm = pe.matmul((m4, m5)[h // 2][:, (h % 2) * T:(h % 2 + 1) * T],
                                               tri_b[:, kt * 4 + h, :], tri[:, kt, :], start=kt == 0, stop=kt == 1)
                        mm.then_inc(S["cum_ready"], 1)
                    if k == 11:
                        pe.wait_ge(S["pooled"], l + 1)
                        wp = pc("w_pool").rearrange("p (a n) -> p a n", a=2)
                        for c in range(2):
                            mm = pe.matmul(m6[:, c * T:(c + 1) * T], wp[:, c, :], rot_tmp[:, c, :], start=True, stop=True)
                        mm.then_inc(S["pool_mm"], 1)
                    if k == 13:
                        pe.wait_ge(S["rot_in"], l + 1)
                        pe.wait_ge(S["bias_ready"], l + 1)
                        for c in range(4):
                            mm = pe.matmul((m4, m5)[c // 2][:, (c % 2) * T:(c % 2 + 1) * T], cc("rot"), rot_raw[:, c, :],
                                           start=True, stop=True)
                        mm.then_inc(S["rot_mm"], 1)
                for k in range(16, N_PROJ, 2):
                    pair_n(hb, k, vb, k, rb, raw_of(k), u_hi, u_lo)
                with pe.Fori(0, 4) as i:
                    hi_, vi_, ri_ = hb + 2 * i, vb + 2 * i, rb + 4 * i
                    hc = l * 8 + 2 * i

                    def gate(k):
                        unit_t(hi_, H1_GATE + k, vi_, V1_GATE + k, ri_, raw_of(H1_GATE + k), u_hi, u_lo)

                    def score(h):
                        b = slice(HD * h, HD * (h + 1))
                        if h == 0:
                            pe.wait_ge(S["staged"], l * 4 + i + 1)
                        pe.wait_ge(S["sneg_ready"], hc + h)
                        pe.matmul(m4[:, 0:P], q_st[b, 0:P], k_st[b, 0:P], start=True, stop=True)
                        pe.matmul(m4[:, P:3 * P], q_st[b, P:T], k_st[b, :], start=True, stop=True)\
                            .then_inc(S["scores"], 1)

                    def turn(h):
                        pe.wait_ge(S["probs_ready"], hc + h + 1)
                        pe.wait_ge(S["probs_t_sb"], hc + h)
                        for j in range(3):
                            mm = pe.transpose(m5[:, j * P:(j + 1) * P], sneg[:, h, j * P:(j + 1) * P], ident[:, :])
                        mm.then_inc(S["probs_t"], 1)

                    def values(h):
                        b = slice(HD * h, HD * (h + 1))
                        pe.wait_ge(S["probs_t_sb"], hc + h + 1)
                        if h == 0:
                            pe.wait_ge(S["o_stored"], l * 4 + i)
                            pe.wait_ge(S["y_local"], l + 1)
                        pe.matmul(m6[b, 0:T], v_st[:, 0, b], pt[:, h, 0:T], start=True, stop=False)
                        pe.matmul(m6[b, P:T], v_st[:, 1, b], pt[:, h, T:3 * P], start=False, stop=True)\
                            .then_inc(S["pv_done"], 1)

                    gate(0)
                    score(0)
                    gate(1)
                    score(1)
                    gate(2)
                    turn(0)
                    gate(3)
                    turn(1)
                    values(0)
                    gate(4)
                    values(1)
                    for k in range(5, 8):
                        gate(k)
                pe.wait_ge(S["o_stored"], 4 * l + 4)
                for c in range(KC):
                    hs, _ = at(hb, H1_BRANCH + c)
                    wait_split(rb, raw_of(H1_BRANCH + c))
                    for n in range(4):
                        vs, vc = at(vb, V1_BRANCH + 2 * c + n // 2)
                        if n % 2 == 0:
                            pe.wait_ge(psum_used[vs], vc)
                        for k in range(2):
                            kk = 2 * n + k
                            mm = three(ps[vs][:, (n % 2) * T:(n % 2 + 1) * T],
                                             lambda w, s, kk=kk: w[:, s, kk * P:(kk + 1) * P],
                                             a_hi[:, kk, :], a_lo[:, kk, :], hs, k == 0, k == 1)
                    mm.then_inc(mm_done[hs], 1)
                for c in range(KC):
                    unit_t(hb, H1_WO + c, vb, V1_WO + c, rb, raw_of(H1_WO + c), u_hi, u_lo,
                           (lambda k: pe.wait_ge(S["merged"], 8 * l + k + 1)) if c == 0 else None)

                def wo_taken(c):
                    vs, vc = at(vb, V1_WO + c)
                    pe.wait_ge(psum_used[vs], vc + 1)

                mean(4 * l + 1, wo_taken)
                variance(4 * l + 1)
                mean(4 * l + 2, lambda c: pe.wait_ge(S["x_chunk"], 24 * l + 8 + c + 1))
                variance(4 * l + 2)
                pe.wait_ge(S["ln_sd"], 4 * l + 3)
                for bank in (m4, m5, m6, m7):
                    pe.matmul(bank[:, :], zeros[:, 0:P], zeros[:, :], start=True, stop=False, skip_group_check=True)
                pe.wait_ge(S["u_lo_made"], 8 * l + 8)
                settled(pe)
                with pe.Fori(0, 4) as i:
                    hi_, vi_, ri_ = hb + 4 * i, vb + 2 * i, rb + 5 * i
                    for t in range(2):
                        h0, v0 = H1_FFN + 8 * t, V1_FFN + 4 * t
                        for k in range(4):
                            unit_t(hi_, h0 + k, vi_, v0 + k, ri_, raw_of(h0 + k), u_hi, u_lo)
                        for k in range(4):
                            hs, _ = at(hi_, h0 + 4 + k)
                            wait_split(ri_, raw_of(h0 + 4 + k))
                            pe.wait_ge(S["h_ready"], 32 * l + 8 * i + 4 * t + k + 1)
                            for c in range(KC):
                                mm = three(ps[4 + c // 2][:, (c % 2) * T:(c % 2 + 1) * T],
                                           lambda w, s, c=c: w[:, s, c * P:(c + 1) * P],
                                           a_hi[:, k, :], a_lo[:, k, :], hs, False, False)
                            mm.then_inc(mm_done[hs], 1)
                for bank in (m4, m5, m6, m7):
                    mm = pe.matmul(bank[:, :], zeros[:, 0:P], zeros[:, :], start=False, stop=True, skip_group_check=True)
                mm.then_inc(S["ffn_done"], 1)
                mean(4 * l + 3, lambda c: pe.wait_ge(S["x_chunk"], 24 * l + 16 + max(c, 1) + 1))
                variance(4 * l + 3)

            h2_0, v2_0, r2_0 = DEPTH * (H1 // 4), DEPTH * (V1 // 4), (R0 + DEPTH * R1) // 4
            pe.wait_ge(S["layer_end"], DEPTH)
            pe.wait_ge(S["tab_ready"], 1)
            pe.wait_ge(S["hot_in"], 48)
            pe.matmul(m4[0:NSA_HEADS, 0:HOT_ROW], table, hot_row, start=True, stop=True).then_inc(S["fn_mm"], 1)
            for j in range(2 * CMP):
                mm = pe.matmul(m6[:, j * NSA_HEADS:(j + 1) * NSA_HEADS], hot_sb[:, j * P:(j + 1) * P], table,
                               start=True, stop=True)
            mm.then_inc(S["bc_mm"], 1)
            pe.wait_ge(S["bias_in"], 16)
            pe.wait_ge(S["fn_sb"], 1)
            for j in range(8):
                if j >= 2:
                    pe.wait_ge(S["flipped"], j - 1)
                pe.matmul((m4, m5)[j % 2][:, :], flip, bias2[:, 2 * j:2 * j + 2, :], start=True, stop=True)\
                  .then_inc(S["flip_mm"], 1)
            pe.wait_ge(S["flipped"], 8)
            with pe.Fori(0, DEPTH) as l:
                hb, vb, rb = h2_0 + l * (H2 // 4), v2_0 + l * (V2 // 4), r2_0 + l * (R2 // 4)
                n_rms = 4 * DEPTH + 2 * l
                n_u = 2 * DEPTH + 2 * l
                variance(n_rms, sq2)
                for k in range(4):
                    unit_t(hb, k, vb, k, rb, k, u_hi, u_lo,
                           (lambda c: pe.wait_ge(S["u_lo_made"], 4 * n_u + c // 2 + 1)) if k == 0 else None)
                pair_n(hb, 4, vb, 4, rb, 4, u_hi, u_lo)
                vs, vc = at(vb, V2_GATE)
                pe.wait_ge(psum_used[vs], vc)
                pe.wait_ge(S["wg_ready"], l + 1)
                for t in range(2):
                    o = ps[vs][:, 48 * t:48 * t + 48]
                    for kc in range(KC):
                        uh, ul = u_hi[:, kc, t * P:(t + 1) * P], u_lo[:, kc, t * P:(t + 1) * P]
                        pe.matmul(o, uh, wg_hi[:, kc, :], start=kc == 0, stop=False)
                        pe.matmul(o, uh, wg_lo[:, kc, :], start=False, stop=False)
                        mm = pe.matmul(o, ul, wg_hi[:, kc, :], start=False, stop=kc == KC - 1)
                mm.then_inc(S["g_tanh"], 1)
                vs, vc = at(vb, V2_HID)
                pe.wait_ge(psum_used[vs], vc)
                pe.wait_ge(S["x2_split"], l + 1)
                for kind in range(2):
                    for j in range(4):
                        h = H2_CMP + 4 * kind + j
                        hs, _ = at(hb, h)
                        wait_split(rb, h)
                        o = ps[vs][0:2 * CMP, T * kind:T * (kind + 1)]
                        for k in range(4):
                            wh, wl = (w[:, hs, k * T:(k + 1) * T] for w in (w_hi, w_lo))
                            xh, xl = (v[:, kind, 4 * j + k, :] for v in (x2_hi, x2_lo))
                            pe.matmul(o, xh, wh, start=j + k == 0, stop=False)
                            pe.matmul(o, xh, wl, start=False, stop=False)
                            mm = pe.matmul(o, xl, wh, start=False, stop=j + k == 6)
                        mm.then_inc(mm_done[hs], 1)
                pe.drain().then_inc(S["cmp_hid"], 1)
                for k in range(KC):
                    unit_t(hb, H2_Q + k, vb, H2_Q + k + V2_SHIFT, rb, H2_Q + k, u_hi, u_lo)
                    if k == 0:
                        pe.wait_ge(S["hid_ready"], l + 1)
                        settled(pe)
                        for j in range(4):
                            mm = pe.transpose(m6[:, 256 + 30 * j:286 + 30 * j], gx[:, j * P:(j + 1) * P],
                                              ident[0:2 * CMP, 0:2 * CMP])
                        mm.then_inc(S["hid_turned"], 1)
                    if k == 1:
                        pe.wait_ge(S["hx_ready"], l + 1)
                        w2k = p2("w2k").rearrange("p (m n) -> p m n", m=2)
                        w2v = p2("w2v").rearrange("p (m n) -> p m n", m=2)
                        for m in range(2):
                            pe.matmul(m5[:, 0:30], w2k[:, m, :], hx[:, 30 * m:30 * m + 30], start=m == 0, stop=m == 1)
                        for g in range(2):
                            for m in range(2):
                                o = 60 + 30 * m + CMP * g
                                mm = pe.matmul(m5[0:CMP, 64 + 64 * g:128 + 64 * g], hx[:, o:o + CMP], w2v[:, m, :],
                                               start=m == 0, stop=m == 1)
                        mm.then_inc(S["cmp_w2"], 1)
                    if k == 2:
                        pe.wait_ge(S["cmp_kv"], l + 1)
                        pe.wait_ge(S["bc_ready"], 1)
                        pe.matmul(m6[:, 0:P], c2("rep")[0:CMP, :], vcn, start=True, stop=True).then_inc(S["vrep"], 1)
                pe.wait_ge(S["q_all"], l + 1)
                for t in range(2):
                    for h in range(NSA_HEADS):
                        b, g = half(h % 2), h // 8
                        o = (t * 8 + h // 2) * CMP
                        mm = pe.matmul((m4, m5)[h % 2][:, o:o + CMP], qn[b, h // 2, t * P:(t + 1) * P], kct[b, CMP * g:CMP * (g + 1)],
                                       start=True, stop=True)
                mm.then_inc(S["cmp_sc"], 1)
                pe.wait_ge(S["bias_in"], 16)
                pe.wait_ge(S["cmp_neg"], l + 1)
                pe.wait_ge(S["vbd_ready"], l + 1)
                pe.wait_ge(S["kv_ready"], 2 * l + 2)
                settled(pe)
                for g in range(NSA_GROUPS):
                    with pe.Fori(0, 4) as i:
                        hi_, vi_, ri_ = hb + i, vb + i, rb + i
                        hc = l * NSA_HEADS + 8 * g + 2 * i

                        def unit(k):
                            h = (H2_QK, H2_V)[g] + k
                            if g == 0:
                                unit_t(hi_, h, vi_, h + V2_SHIFT, ri_, h, u_hi, u_lo)
                            elif k % 2 == 0:
                                pair_n(hi_, h, vi_, h + V2_SHIFT, ri_, h, u_hi, u_lo)

                        def score(h):
                            b = half(h)
                            pe.wait_ge(S["n_sneg"], 2 * (hc + h))
                            kk = kdup[b, 2 * g:2 * g + 2, :]
                            pe.matmul(m5[:, 0:T].rearrange("p (a n) -> p a n", a=2), q_st2[b, 0:P], kk[:, :, 0:P],
                                      start=True, stop=True)
                            pe.matmul(m4[:, :].rearrange("p (a n) -> p a n", a=2), q_st2[b, P:T], kk,
                                      start=True, stop=True).then_inc(S["n_scores"], 1)

                        def turn(h, kind):
                            n = 2 * (hc + h) + kind
                            pe.wait_ge(S["n_probs"], n + 1)
                            pe.wait_ge(S["n_pt"], n)
                            for j in range(3):
                                mm = pe.transpose(m6[:, j * P:(j + 1) * P], sn[:, 2 * h + kind, j * P:(j + 1) * P],
                                                  ident[:, :])
                            mm.then_inc(S["n_turn"], 1)

                        def values(h, kind):
                            b, n = half(h), 2 * (hc + h) + kind
                            pe.wait_ge(S["n_pt"], n + 1)
                            if h == 0 and kind == 0:
                                pe.wait_ge(S["o2_stored"], 8 * l + 4 * g + i)
                            pe.matmul(m7[b, 0:T], vnat[:, kind, 0, half(g)], pt2[:, kind, 0:T], start=kind == 0, stop=False)
                            pe.matmul(m7[b, P:T], vnat[:, kind, 1, half(g)], pt2[:, kind, T:384], start=False,
                                      stop=kind == 1).then_inc(S["n_pv"], 1)

                        pe.wait_ge(S["staged2"], 8 * l + 4 * g + i + 1)
                        score(0)
                        unit(0)
                        score(1)
                        turn(0, 0)
                        unit(1)
                        values(0, 0)
                        turn(0, 1)
                        unit(2)
                        values(0, 1)
                        turn(1, 0)
                        unit(3)
                        values(1, 0)
                        turn(1, 1)
                        values(1, 1)
                pe.wait_ge(S["cmp_p"], l + 1)
                for t in range(2):
                    for g in range(2):
                        mm = pe.transpose(m6[:, g * T + t * P:g * T + (t + 1) * P], pc_n[:, t, 8 * g:8 * g + 8, :], ident[:, :])
                mm.then_inc(S["cmp_turn"], 1)
                pe.wait_ge(S["o2_stored"], 8 * l + 8)
                pe.wait_ge(S["cmp_pt"], l + 1)
                for c in range(KC):
                    mm = pe.matmul(ps[4 + c // 2][:, (c % 2) * T:(c % 2 + 1) * T], vbd[:, c // 4, 2 * (c % 4):2 * (c % 4) + 2, :],
                                   pc_t[:, c // 4, :], start=True, stop=True)
                mm.then_inc(S["cmp_o"], 1)
                pe.wait_ge(S["cmp_stored"], l + 1)
                pe.wait_ge(S["rr_done"], 8 * l + 9)
                pe.wait_ge(S["v_cent"], 4 * l + 4)
                for p in range(2):
                    h0, r0 = H2_PAIR + 16 * p, H2_PAIR + 16 * p
                    nh = 4 * l + 2 * p

                    def g_unit(k):
                        unit_t(hb, h0 + k, vb, h0 + k + V2_SHIFT, rb, r0 + k, u_hi, u_lo)

                    def scores_t(j):
                        bank, c0 = (m4, m5)[j], 2 * (2 * p + j)
                        for kc in range(2):
                            pe.matmul(bank[:, 0:T], rk[:, c0 + kc, 0:P], rq[:, c0 + kc, :], start=kc == 0, stop=kc == 1)
                        for kc in range(2):
                            mm = pe.matmul(bank[:, T:384], rk[:, c0 + kc, P:T], rq[:, c0 + kc, P:T], start=kc == 0,
                                           stop=kc == 1)
                        mm.then_inc(S["r_st"], 1)

                    def out_t(j):
                        pe.wait_ge(S["r_sts"], nh + j + 1)
                        if j == 1:
                            pe.wait_ge(S["r_sts"], nh + 2)
                        for m in range(4):
                            bank, o = ((m6, m7), (m4, m5))[j][m // 2], (m % 2) * T
                            v0 = rv[:, 2 * p + j, 0, m * P:(m + 1) * P]
                            v1 = rv[:, 2 * p + j, 1, m * P:(m + 1) * P]
                            pe.matmul(bank[:, o:o + T], v0, sn[:, j, 0:T], start=True, stop=False)
                            mm = pe.matmul(bank[:, o + P:o + T], v1, sn[:, j, T:384], start=False, stop=True)
                        mm.then_inc(S["r_ot"], 1)

                    def spread(j):
                        pe.wait_ge(S["r_sq"], nh + j + 1)
                        pe.wait_ge(S["r_copy"], nh + j + 1)
                        for m in range(4):
                            mm = pe.matmul((m6, m7)[j][:, 0:T], ones_d[:, :], r4[:, m, :], start=m == 0, stop=m == 3)
                        mm.then_inc(S["r_var"], 1)

                    if p == 1:
                        pe.wait_ge(S["r_norm"], nh)
                    scores_t(0)
                    scores_t(1)
                    g_unit(0)
                    out_t(0)
                    g_unit(1)
                    out_t(1)
                    g_unit(2)
                    spread(0)
                    g_unit(3)
                    spread(1)
                    for k in range(4, 8):
                        g_unit(k)
                    for c in range(KC):
                        unit_t(hb, h0 + 8 + c, vb, h0 + 8 + c + V2_SHIFT, rb, r0 + 8 + c, a_hi, a_lo,
                               (lambda k: pe.wait_ge(S["y_full"], 16 * l + 8 * p + k + 1)) if c == 0 else None)
                for k in range(2 * KC):
                    unit_t(hb, H2_MA + k, vb, H2_MA + k + V2_SHIFT, rb, H2_MA + k, u_hi, u_lo)
                for c in range(KC):
                    unit_t(hb, H2_ONSA + c, vb, H2_ONSA + c + V2_SHIFT, rb, H2_ONSA + c, a_hi, a_lo,
                           (lambda k: pe.wait_ge(S["nsa_full"], 4 * l + k // 2 + 1)) if c == 0 else None)
                for c in range(KC):
                    unit_t(hb, H2_OUT + c, vb, H2_OUT + c + V2_SHIFT, rb, H2_OUT + c, u_hi, u_lo,
                           (lambda k: pe.wait_ge(S["merged"], 8 * DEPTH + 8 * l + k + 1)) if c == 0 else None)
                variance(n_rms + 1, sq2)
                pe.wait_ge(S["ln_sd"], n_rms + 2)
                for bank in (m4, m5, m6, m7):
                    pe.matmul(bank[:, :], zeros[:, 0:P], zeros[:, :], start=True, stop=False, skip_group_check=True)

                def ffn(hx_, vx_, rx_, h0, v0, order, n0):
                    v = v0
                    for idx, (what, k) in enumerate(order):
                        h = h0 + idx
                        if what != "d":
                            unit_t(hx_, h, vx_, v, rx_, h, u_hi, u_lo)
                            v += 1
                            continue
                        wait_split(rx_, h)
                        pe.wait_ge(S["h_ready"], n0 + k + 1)
                        hs, _ = at(hx_, h)
                        for c in range(KC):
                            mm = three(ps[4 + c // 2][:, (c % 2) * T:(c % 2 + 1) * T],
                                       lambda w, s, c=c: w[:, s, c * P:(c + 1) * P],
                                       a_hi[:, k, :], a_lo[:, k, :], hs, False, False)
                        mm.then_inc(mm_done[hs], 1)

                pe.wait_ge(S["u_lo_made"], 4 * n_u + 8)
                settled(pe)
                n_h = 32 * DEPTH + FFN2 * l
                with pe.Fori(0, 5) as i:
                    ffn(hb + 3 * i, vb + 2 * i, rb + 3 * i, H2_FFN, V2_FFN, BODY2, n_h + 4 * i)
                ffn(hb, vb, rb, H2_FFN + 60, V2_FFN + 40, TAIL2, n_h + 20)
                for bank in (m4, m5, m6, m7):
                    mm = pe.matmul(bank[:, :], zeros[:, 0:P], zeros[:, :], start=False, stop=True, skip_group_check=True)
                mm.then_inc(S["ffn_done"], 1)
            variance(6 * DEPTH, sq2)

        @block.scalar
        def _(act):
            def split_hi(hb, ho, rb, ro):
                hs, hcnt = at(hb, ho)
                rsl, rc = at(rb, ro)
                act.wait_ge(landed[rsl], 16 * (rc + 1))
                act.wait_ge(mm_done[hs], hcnt)
                act.activation(w_hi[:, hs, :], raw[:, rsl, :], ACT.Copy).then_inc(hi_made[hs], 1)

            def squares(n):
                for p in range(4):
                    act.wait_ge(S["ln_cent"], 4 * n + p + 1)
                    act.activation(sq[:, 2 * p:2 * p + 2, :], y[:, 2 * p:2 * p + 2, :], ACT.Square).then_inc(S["ln_sq"], 1)
                act.wait_ge(S["ln_var"], n + 1)
                act.activation(sd[:, :], m5[:, 0:T], ACT.Sqrt, bias=eps[:, 0:1]).then_inc(S["ln_sd"], 1)

            def lead_u1(n, b):
                for p in range(4):
                    for c in (2 * p, 2 * p + 1):
                        act.wait_ge(S["ln_scaled"], 8 * n + c + 1)
                        ins = act.activation(u_hi[:, c, :], y[:, c, :], ACT.Identity, bias=b[:, c:c + 1])
                    ins.then_inc(S["u_hi_made"], 1)

            def new_x(n, b):
                for c in range(KC):
                    act.wait_ge(S["x_scaled_out"], 8 * n + c + 1)
                    act.activation(x[:, c, :], y[:, c, :], ACT.Identity, bias=b[:, c:c + 1]).then_inc(S["x_chunk"], 1)

            def lead_u(n):
                for p in range(4):
                    act.wait_ge(S["ln_mod"], 4 * (n - 2 * DEPTH) + p + 1)
                    act.activation(u_hi[:, 2 * p:2 * p + 2, :], y[:, 2 * p:2 * p + 2, :], ACT.Copy)\
                       .then_inc(S["u_hi_made"], 1)

            act.dma_start(c_row, c_in.partition_broadcast(P)).then_inc(S["c_in"], 16)
            act.dma_start(x[:, :, :], x_in).then_inc(S["x_in"], 16)
            act.dma_start(con, con1).then_inc(S["con_in"], 16)
            act.dma_start(ident[:, :], ident_in).then_inc(S["ident_in"], 16)
            act.dma_start(pos_i.bitcast(I32), positions.partition_broadcast(P)).then_inc(S["pos_in"], 16)
            act.wait_ge(S["c_in"], 16)
            act.activation(c_tmp, c_row, ACT.Tanh, scale=0.5).then_inc(S["c_tanh"], 1)
            act.wait_ge(S["setup_dve"], 1)
            act.activation(sin, ang[:, 2, :], ACT.Sin)
            act.activation(cos, ang[:, 3, :], ACT.Sin).then_inc(S["sin_ready"], 1)
            for k in range(AHEAD):
                split_hi(0, k, R0 // 4, k)
            with act.Fori(0, DEPTH) as l:
                hb, vb, rb = l * (H1 // 4), l * (V1 // 4), R0 // 4 + l * (R1 // 4)

                def ahead(k):
                    split_hi(hb, k + AHEAD, rb, raw_of(k + AHEAD))

                act.wait_ge(S["layer_end"], l)
                settled(act)
                act.dma_start(par[:, 0:NPAR1], par1[l]).then_inc(S["par_in"], 16)
                act.wait_ge(S["par_in"], 16 * (l + 1))
                act.activation(wf_hi[:, :, :], pc("w_f").rearrange("p (c n) -> p c n", n=4), ACT.Copy)\
                   .then_inc(S["wf_hi"], 1)
                act.activation(bgh[:, 0:32], pc("b_gate"), ACT.Copy, scale=0.5)
                act.activation(bgh[:, 32:40], pc("b_proj")[:, 8:16], ACT.Copy, scale=-SCORE_SCALE)
                act.drain()
                squares(4 * l)
                lead_u1(2 * l, ada[:, 0:8])
                for k in range(16):
                    ahead(k)
                    hs, hcnt = at(hb, k)
                    vs, _ = at(vb, k)
                    act.wait_ge(mm_done[hs], hcnt + 1)
                    if k < 8:
                        dst, b, sc = proj[:, k, :], pc("b_proj")[:, k:k + 1], 1.0
                    else:
                        j = k - 8
                        is_q = j % 4 < 2
                        b = bgh[:, 32 + j:33 + j] if is_q else pc("b_proj")[:, k:k + 1]
                        sc = -SCORE_SCALE if is_q else 1.0
                        dst = rot_raw[:, j, :] if j < 4 else qk[:, (2 if is_q else 6) + j % 2, :]
                    act.activation(dst, ps[vs][:, 0:T], ACT.Identity, bias=b, scale=sc).then_inc(psum_used[vs], 1)
                    if k == 2:
                        act.wait_ge(S["f_abs"], l + 1)
                        act.activation(small[:, 24:32], small[:, 8:16], ACT.Exp, scale=-1.0)
                        act.drain()
                        act.activation(small[:, 32:40], small[:, 24:32], ACT.Ln, bias=1.0).then_inc(S["f_log"], 1)
                    if k == 7:
                        act.drain().then_inc(S["conv_in"], 1)
                    if k == 11:
                        act.drain().then_inc(S["rot_in"], 1)
                act.drain().then_inc(S["proj_all"], 1)
                for k in range(16, N_PROJ):
                    ahead(k)
                with act.Fori(0, 4) as i:
                    hi_, vi_, ri_ = hb + 2 * i, vb + 2 * i, rb + 4 * i
                    hc = l * 8 + 2 * i

                    def gate(k):
                        split_hi(hi_, H1_GATE + k + AHEAD, ri_, raw_of(H1_GATE + k + AHEAD))
                        hs, hcnt = at(hi_, H1_GATE + k)
                        vs, _ = at(vi_, V1_GATE + k)
                        act.wait_ge(mm_done[hs], hcnt + 1)
                        act.activation(gates[:, 8 * i + k, :], ps[vs][:, 0:T], ACT.Tanh, bias=bgh[:, bass.ds(8 * i + k, 1)],
                                       scale=0.5).then_inc(psum_used[vs], 1)

                    def exps(h):
                        act.wait_ge(S["sneg_ready"], hc + h + 1)
                        act.activation(sneg[:, h, 0:P], sneg[:, h, 0:P], ACT.Exp, bias=mn[:, h, 0:1], scale=-1.0,
                                       accum_out=rs[:, h, 0:1])
                        act.activation(sneg[:, h, P:3 * P], sneg[:, h, P:3 * P], ACT.Exp, bias=mn[:, h, 1:2], scale=-1.0,
                                       accum_out=rs[:, h, 1:2]).then_inc(S["exp_done"], 1)

                    def turned(h):
                        act.wait_ge(S["probs_t"], hc + h + 1)
                        act.activation(pt[:, h, :], m5[:, 0:384], ACT.Copy).then_inc(S["probs_t_sb"], 1)

                    gate(0)
                    exps(0)
                    gate(1)
                    exps(1)
                    gate(2)
                    turned(0)
                    gate(3)
                    turned(1)
                    gate(4)
                    act.wait_ge(S["pv_done"], hc + 2)
                    act.activation(a_hi[:, 4 + i, :], m6[:, 0:T], ACT.Copy).then_inc(S["o_hi_made"], 1)
                    for k in range(5, 8):
                        gate(k)
                act.drain().then_inc(S["gates_ready"], 1)

                def lead_merged(c):
                    act.wait_ge(S["msum_ready"], 8 * l + c + 1)
                    act.activation(u_hi[:, c, :], msum[:, c % 2, 2, :], ACT.Copy, scale=0.5).then_inc(S["m_hi_made"], 1)

                for c in range(KC):
                    ahead(H1_BRANCH + c)
                    if c:
                        lead_merged(c - 1)
                lead_merged(KC - 1)
                for c in range(KC):
                    ahead(H1_WO + c)
                squares(4 * l + 1)
                new_x(2 * l, pc("ln1_b"))
                squares(4 * l + 2)
                lead_u1(2 * l + 1, ada[:, 24:32])
                with act.Fori(0, 4) as i:
                    hi_, vi_, ri_ = hb + 4 * i, vb + 2 * i, rb + 5 * i
                    for k in range(16):
                        split_hi(hi_, H1_FFN + k + AHEAD, ri_, raw_of(H1_FFN + k + AHEAD))
                        t, j = k // 8, k % 8
                        if j >= 4:
                            continue
                        hs, hcnt = at(hi_, H1_FFN + k)
                        vs, _ = at(vi_, V1_FFN + 4 * t + j)
                        act.wait_ge(mm_done[hs], hcnt + 1)
                        act.activation(tmpa[:, j % 2, :], ps[vs][:, 0:T], ACT.Relu,
                                       bias=pc("b_up")[:, bass.ds(8 * i + 4 * t + j, 1)]).then_inc(psum_used[vs], 1)
                        act.drain()
                        act.activation(y[:, j, :], tmpa[:, j % 2, :], ACT.Square)
                        act.activation(a_hi[:, j, :], tmpa[:, j % 2, :], ACT.Square).then_inc(S["h_hi_made"], 1)
                squares(4 * l + 3)
                new_x(2 * l + 1, pc("ln2_b"))
                act.drain().then_inc(S["layer_end"], 1)
            act.wait_ge(S["layer_end"], DEPTH)
            act.dma_start(table[0:32, :], rel_bias).then_inc(S["table_in"], 16)
            act.dma_start(hot_row, hot[:, 0:HOT_ROW]).then_inc(S["hot_in"], 16)
            act.dma_start(hot_sb, hot[:, HOT_ROW:]).then_inc(S["hot_in"], 16)
            act.dma_start(flip, flip_in).then_inc(S["hot_in"], 16)
            act.dma_start(con_2, con2).then_inc(S["con2_in"], 16)
            act.wait_ge(S["fn_mm"], 1)
            act.activation(fn_sb, m4[0:NSA_HEADS, 0:HOT_ROW], ACT.Copy).then_inc(S["fn_sb"], 1)
            act.wait_ge(S["fn_sb"], 1)
            act.dma_start(fn_dram, fn_sb).then_inc(S["fn_out"], 16)
            act.wait_ge(S["fn_out"], 16)
            act.dma_start(bias2, bass.AP(fn_dram.tensor, 0, [[1, P], [HOT_ROW, NSA_HEADS], [1, T]]))\
               .then_inc(S["bias_in"], 16)
            act.wait_ge(S["con2_in"], 16)

            def squares2(n, ready):
                for p in range(4):
                    ready(p)
                    act.activation(sq2[:, 2 * p:2 * p + 2, :], x[:, 2 * p:2 * p + 2, :], ACT.Square).then_inc(S["ln_sq"], 1)
                act.wait_ge(S["ln_var"], n + 1)
                act.activation(sd[:, :], m5[:, 0:T], ACT.Sqrt, bias=eps[:, 1:2]).then_inc(S["ln_sd"], 1)

            h2_0, v2_0, r2_0 = DEPTH * (H1 // 4), DEPTH * (V1 // 4), (R0 + DEPTH * R1) // 4
            with act.Fori(0, DEPTH) as l:
                hb, vb, rb = h2_0 + l * (H2 // 4), v2_0 + l * (V2 // 4), r2_0 + l * (R2 // 4)
                n_rms = 4 * DEPTH + 2 * l
                n_u = 2 * DEPTH + 2 * l

                def ahead(k):
                    split_hi(hb, k + AHEAD, rb, k + AHEAD)

                def wait_mm(h, b=None):
                    hs, hcnt = at(hb if b is None else b, h)
                    act.wait_ge(mm_done[hs], hcnt + 1)

                def bank_of(h, b=None):
                    return at(vb if b is None else b, h)[0]

                act.wait_ge(S["x_ready2"], l + 1)
                act.dma_start(par[:, 0:NPAR2], par2[l]).then_inc(S["par2_in"], 16)
                squares2(n_rms, lambda p: None)
                act.wait_ge(S["par2_in"], 16 * (l + 1))
                act.activation(wg_hi, p2("w_gate").rearrange("p (c n) -> p c n", n=48), ACT.Copy).then_inc(S["wg_hi"], 1)
                lead_u(n_u)
                for k in range(N_KV):
                    ahead(k)
                    if k == 4:
                        act.wait_ge(S["x2_ready"], l + 1)
                        act.activation(x2_hi, x2, ACT.Copy).then_inc(S["x2_hi"], 1)
                        continue
                    wait_mm(k)
                    bank = ps[bank_of(k)]
                    if k == 0:
                        act.wait_ge(S["bc_ready"], 1)
                    if k < 2:
                        for g in range(2):
                            for a in range(2):
                                v = bank[half(g), a:a + 1]
                                src = bass.AP(v.tensor, v.offset, [[v.ap[0][0], HD], [2, CMP_LC], [CMP_STRIDE, CMP]])
                                ins = act.activation(x2[half(a), k, :, CMP * g:CMP * (g + 1)], src, ACT.Copy)
                        ins.then_inc(psum_used[bank_of(k)], 1)
                        if k == 1:
                            act.drain().then_inc(S["x2_raw"], 1)
                    elif k < 4:
                        kind = 3 - k
                        for g in range(2):
                            for a in range(2):
                                ins = act.activation(kdup[half(a), 2 * g + kind, :], bank[half(g), 0:T], ACT.Copy)
                        ins.then_inc(psum_used[bank_of(k)], 1)
                    else:
                        for t in range(2):
                            act.activation(vnat[:, :, t, :], ps[bank_of(4 + t)][:, 0:T].rearrange("p (a n) -> p a n", a=2),
                                           ACT.Copy).then_inc(psum_used[bank_of(4 + t)], 1)
                act.drain().then_inc(S["kv_ready"], 1)
                act.wait_ge(S["g_tanh"], l + 1)
                act.activation(gsig.rearrange("p t h j -> p (t h j)"), ps[bank_of(V2_GATE)][:, 0:96], ACT.Tanh, scale=0.5)\
                   .then_inc(psum_used[bank_of(V2_GATE)], 1)
                act.drain().then_inc(S["kv_ready"], 1)
                for k in range(N_CMP):
                    ahead(H2_CMP + k)
                act.wait_ge(S["gelu_in"], l + 1)
                act.activation(gz, gy, ACT.Tanh, scale=GELU_SCALE).then_inc(S["gelu_t"], 1)
                for k in range(KC):
                    ahead(H2_Q + k)
                    wait_mm(H2_Q + k)
                    v = bank_of(H2_Q + k + V2_SHIFT)
                    act.activation(qn[:, k, :], ps[v][:, 0:T], ACT.Copy, scale=-SCORE_SCALE).then_inc(psum_used[v], 1)
                act.drain().then_inc(S["q_all"], 1)
                act.wait_ge(S["cmp_neg"], l + 1)
                act.activation(sc_cmp, sc_cmp, ACT.Exp, scale=-1.0).then_inc(S["cmp_exp"], 1)
                for g in range(NSA_GROUPS):
                    with act.Fori(0, 4) as i:
                        hi_, vi_, ri_ = hb + i, vb + i, rb + i
                        hc = l * NSA_HEADS + 8 * g + 2 * i
                        nb = 4 * l + i

                        def unit_ahead(k):
                            h = (H2_QK, H2_V)[g] + k + AHEAD
                            split_hi(hi_, h, ri_, h)

                        def unit_out(k):
                            h = (H2_QK, H2_V)[g] + k
                            wait_mm(h, hi_)
                            v = bank_of(h + V2_SHIFT, vi_)
                            if g == 0:
                                if k % 2 == 0:
                                    act.wait_ge(S["rr_done"], 2 * nb + k // 2)
                                act.activation(r4[:, k, :], ps[v][:, 0:T], ACT.Copy).then_inc(psum_used[v], 1)
                                if k % 2:
                                    act.drain().then_inc(S["rr_ready"], 1)
                            elif k % 2:
                                for t in range(2):
                                    v = bank_of(h - 1 + t + V2_SHIFT, vi_)
                                    act.activation(rv[:, i, t, (k - 1) * P:(k + 1) * P], ps[v][:, 0:T], ACT.Copy)\
                                       .then_inc(psum_used[v], 1)
                                if k == 3:
                                    act.drain().then_inc(S["v_ready"], 1)

                        def exps(h):
                            for kind in range(2):
                                act.wait_ge(S["n_sneg"], 2 * (hc + h) + kind + 1)
                                j = 2 * h + kind
                                act.activation(sn[:, j, 0:P], sn[:, j, 0:P], ACT.Exp, bias=mn2[:, j, 0:1], scale=-1.0,
                                               accum_out=rs2[:, j, 0:1])
                                act.activation(sn[:, j, P:384], sn[:, j, P:384], ACT.Exp, bias=mn2[:, j, 1:2], scale=-1.0,
                                               accum_out=rs2[:, j, 1:2]).then_inc(S["n_exp"], 1)

                        def turned(h, kind):
                            act.wait_ge(S["n_turn"], 2 * (hc + h) + kind + 1)
                            act.wait_ge(S["n_pv"], 2 * hc if h == 0 else 2 * hc + kind + 1)
                            act.activation(pt2[:, kind, :], m6[:, 0:384], ACT.Copy).then_inc(S["n_pt"], 1)

                        unit_ahead(0)
                        exps(0)
                        unit_out(0)
                        unit_ahead(1)
                        exps(1)
                        turned(0, 0)
                        unit_out(1)
                        unit_ahead(2)
                        turned(0, 1)
                        unit_out(2)
                        unit_ahead(3)
                        turned(1, 0)
                        unit_out(3)
                        turned(1, 1)
                        act.wait_ge(S["n_pv"], 2 * hc + 4)
                        act.activation(y[:, 4 * g + i, :], m7[:, 0:T], ACT.Copy).then_inc(S["o2_stored"], 1)
                act.wait_ge(S["cmp_turn"], l + 1)
                act.activation(pc_t.rearrange("p g q -> p (g q)"), m6[:, :], ACT.Copy).then_inc(S["cmp_pt"], 1)
                for p in range(2):
                    h0 = H2_PAIR + 16 * p
                    nh = 4 * l + 2 * p

                    def r_squares(j):
                        act.wait_ge(S["r_copy"], nh + j + 1)
                        if j == 1:
                            act.wait_ge(S["r_var"], nh + 1)
                        o = rv[:, 2 * p + j, :, :].rearrange("p a (b t) -> p (a b) t", t=T)
                        act.activation(r4, o, ACT.Square).then_inc(S["r_sq"], 1)

                    def r_root(j):
                        act.wait_ge(S["r_var"], nh + j + 1)
                        act.activation((sd[:, :], rt[:, 0, :])[j], (m6, m7)[j][:, 0:T], ACT.Sqrt, bias=eps[:, 2:3], scale=4.0 * D / RET_DV)\
                           .then_inc(S["r_sd"], 1)

                    def lead_y(c):
                        act.wait_ge(S["y_ready"], 16 * l + 8 * p + c + 1)
                        act.activation(a_hi[:, c, :], pt2[:, c % 2, 0:T], ACT.Copy).then_inc(S["y_hi"], 1)

                    for k in range(8):
                        ahead(h0 + k)
                        wait_mm(h0 + k)
                        if k >= 2:
                            act.wait_ge(S["sg_ready"], 16 * l + 8 * p + k - 1)
                        v = bank_of(h0 + k + V2_SHIFT)
                        act.activation(tmpa[:, k % 2, :], ps[v][:, 0:T], ACT.Tanh, scale=0.5).then_inc(S["g2_tanh"], 1)
                        if k == 1:
                            r_squares(0)
                        if k == 3:
                            r_squares(1)
                        if k == 4:
                            r_root(0)
                            r_root(1)
                    lead_y(0)
                    lead_y(1)
                    ahead(h0 + 8)
                    lead_y(2)
                    lead_y(3)
                    ahead(h0 + 9)
                    for c in range(4, KC):
                        lead_y(c)
                    for c in range(KC):
                        if c >= 2:
                            ahead(h0 + 8 + c)
                        if p == 0:
                            if c >= 1:
                                wait_mm(h0 + 8 + c - 1)
                                v = bank_of(h0 + 8 + c - 1 + V2_SHIFT)
                                act.activation(yret[:, c - 1, :], ps[v][:, 0:T], ACT.Copy).then_inc(psum_used[v], 1)
                    if p == 0:
                        wait_mm(h0 + 15)
                        v = bank_of(h0 + 15 + V2_SHIFT)
                        act.activation(yret[:, 7, :], ps[v][:, 0:T], ACT.Copy).then_inc(psum_used[v], 1)
                for k in range(2 * KC):
                    ahead(H2_MA + k)
                    wait_mm(H2_MA + k)
                    v = bank_of(H2_MA + k + V2_SHIFT)
                    if k < KC:
                        if k >= 2:
                            act.wait_ge(S["ma_all"], 8 * l + k - 1)
                        act.activation(tmpa[:, k % 2, :], ps[v][:, 0:T], ACT.Tanh, scale=0.5).then_inc(psum_used[v], 1)
                        if k % 2:
                            pr = k // 2
                            act.activation(a_hi[:, 2 * pr:2 * pr + 2, :], y[:, 2 * pr:2 * pr + 2, :], ACT.Copy)\
                               .then_inc(S["nsa_hi"], 1)
                    else:
                        act.activation(sig_b[:, k - KC, :], ps[v][:, 0:T], ACT.Tanh, scale=0.5).then_inc(psum_used[v], 1)
                act.drain().then_inc(S["mb_all"], 1)

                def lead_merged(c):
                    act.wait_ge(S["msum_ready"], 8 * DEPTH + 8 * l + c + 1)
                    act.activation(u_hi[:, c, :], pt2[:, c % 2, 0:T], ACT.Copy, scale=0.5).then_inc(S["m_hi_made"], 1)

                for c in range(KC):
                    ahead(H2_ONSA + c)
                    if c:
                        lead_merged(c - 1)
                lead_merged(KC - 1)
                for c in range(KC):
                    ahead(H2_OUT + c)

                def out_taken(p):
                    for c in (2 * p, 2 * p + 1):
                        vs, vc = at(vb, H2_OUT + c + V2_SHIFT)
                        act.wait_ge(psum_used[vs], vc + 1)

                squares2(n_rms + 1, out_taken)
                lead_u(n_u + 1)

                def ffn(hx_, vx_, rx_, h0, v0, order, n0):
                    v = v0
                    for idx, (what, k) in enumerate(order):
                        h = h0 + idx
                        split_hi(hx_, h + AHEAD, rx_, h + AHEAD)
                        if what == "a":
                            hs, hcnt = at(hx_, h)
                            act.wait_ge(mm_done[hs], hcnt + 1)
                            act.activation(pt2[:, k % 2, 0:T], ps[at(vx_, v)[0]][:, 0:T], ACT.Tanh, scale=0.5)\
                               .then_inc(S["t2_made"], 1)
                        if what == "b":
                            vs, vc = at(vx_, v)
                            act.wait_ge(psum_used[vs], vc + 1)
                            act.activation(a_hi[:, k, :], y[:, k, :], ACT.Copy).then_inc(S["h_hi_made"], 1)
                        if what != "d":
                            v += 1

                n_h = 32 * DEPTH + FFN2 * l
                with act.Fori(0, 5) as i:
                    ffn(hb + 3 * i, vb + 2 * i, rb + 3 * i, H2_FFN, V2_FFN, BODY2, n_h + 4 * i)
                ffn(hb, vb, rb, H2_FFN + 60, V2_FFN + 40, TAIL2, n_h + 20)
            act.wait_ge(S["x_ready2"], DEPTH + 1)
            squares2(6 * DEPTH, lambda p: None)
            act.wait_ge(S["y_last"], 1)
            act.dma_start(out, y[:, :, :]).then_inc(S["out_done"], 16)

        @block.vector
        def _(dve):
            def split_lo(hb, ho, rb, ro):
                hs, hcnt = at(hb, ho)
                rsl, _ = at(rb, ro)
                dve.wait_ge(hi_made[hs], hcnt + 1)
                dve.tensor_tensor(w_lo[:, hs, :], raw[:, rsl, :], w_hi[:, hs, :].bitcast(F32), ALU.subtract)\
                   .then_inc(raw_used[rsl], 1)

            def ada_unit(rb, ro, dst):
                rsl, rc = at(rb, ro)
                dve.wait_ge(landed[rsl], 16 * (rc + 1))
                dve.tensor_tensor_reduce(out=raw[:, rsl, :], in0=raw[:, rsl, :], in1=c_row, scale=1.0, scalar=0.0,
                                         op0=ALU.mult, op1=ALU.add, accum_out=dst).then_inc(raw_used[rsl], 1)

            def centre(n):
                dve.wait_ge(S["ln_mean"], n + 1)
                for p in range(4):
                    dve.tensor_tensor(y[:, 2 * p:2 * p + 2, :], x[:, 2 * p:2 * p + 2, :],
                                      m4[:, 0:T].unsqueeze(1).broadcast_to([P, 2, T]), ALU.subtract)\
                       .then_inc(S["ln_cent"], 1)

            def root(n):
                dve.wait_ge(S["ln_sd"], n + 1)
                dve.reciprocal(rstd[:, :], sd[:, :])
                dve.drain()

            def scale_rows(g, name):
                for c in range(KC):
                    dve.scalar_tensor_tensor(out=y[:, c, :], in0=y[:, c, :], scalar=g[:, c:c + 1], in1=rstd[:, :],
                                             op0=ALU.mult, op1=ALU.mult).then_inc(S[name], 1)

            def rest_u1(n, b):
                for p in range(4):
                    dve.wait_ge(S["u_hi_made"], 4 * n + p + 1)
                    for c in (2 * p, 2 * p + 1):
                        ins = dve.scalar_tensor_tensor(out=u_lo[:, c, :], in0=y[:, c, :], scalar=b[:, c:c + 1],
                                                       in1=u_hi[:, c, :].bitcast(F32), op0=ALU.add, op1=ALU.subtract)
                    ins.then_inc(S["u_lo_made"], 1)

            def rest_u(n):
                for p in range(4):
                    dve.wait_ge(S["u_hi_made"], 4 * n + p + 1)
                    sl = slice(2 * p, 2 * p + 2)
                    dve.tensor_tensor(u_lo[:, sl, :], y[:, sl, :], u_hi[:, sl, :].bitcast(F32), ALU.subtract)\
                       .then_inc(S["u_lo_made"], 1)

            dve.memset(ones_d[:, :], 1.0 / D)
            dve.memset(zeros[:, :], 0.0)
            dve.memset(eps[:, 0:1], LN_EPS)
            dve.memset(eps[:, 1:2], RMS_EPS)
            dve.memset(eps[:, 2:3], 4 * GN_EPS)
            dve.memset(mn2[:, :, :], 0.0)
            dve.memset(cs[:, :, 0:POOL_PAD], 0.0)
            dve.memset(vv[:, :, 0:2], 0.0)
            dve.memset(mn[:, :, :], 0.0)
            dve.drain().then_inc(S["consts"], 1)
            dve.wait_ge(S["c_tanh"], 1)
            dve.scalar_tensor_tensor(out=c_tmp, in0=c_tmp, scalar=1.0, in1=c_row, op0=ALU.add, op1=ALU.mult)
            dve.drain()
            dve.tensor_scalar(c_row, c_tmp, 0.5, None, ALU.mult)
            dve.drain()
            dve.wait_ge(S["x_in"], 16)
            for c in range(KC):
                dve.nop().then_inc(S["x_chunk"], 1)
            for j in range(8):
                ada_unit(0, j, ada[:, j:j + 1])
            dve.wait_ge(S["con_in"], 16)
            dve.wait_ge(S["pos_in"], 16)
            dve.tensor_copy(ang[:, 0, :], pos_i.bitcast(I32))
            for h in range(4):
                dve.tensor_copy(bias[:, h, :], cc("mask"))
            dve.drain()
            dve.tensor_scalar(ang[:, 0, :], ang[:, 0, :], cc("inv_freq"), None, ALU.mult)
            dve.drain()
            dve.tensor_scalar(ang[:, 1, :], ang[:, 0, :], 1.0 / (2 * PI), ROUND_MAGIC, ALU.mult, ALU.add)
            dve.drain()
            dve.tensor_scalar(ang[:, 1, :], ang[:, 1, :], ROUND_MAGIC, None, ALU.subtract)
            dve.drain()
            for part in (TWO_PI_A, TWO_PI_B, TWO_PI_C):
                dve.scalar_tensor_tensor(out=ang[:, 0, :], in0=ang[:, 1, :], scalar=-part, in1=ang[:, 0, :],
                                         op0=ALU.mult, op1=ALU.add)
                dve.drain()
            dve.tensor_scalar(ang[:, 2, :], ang[:, 0, :], -SAFE_PI, SAFE_PI, ALU.max, ALU.min)
            dve.tensor_scalar(ang[:, 3, :], ang[:, 0, :], PI / 2, None, ALU.add)
            dve.drain()
            dve.tensor_scalar(ang[:, 1, :], ang[:, 3, :], PI, -2 * PI, ALU.is_gt, ALU.mult)
            dve.drain()
            dve.tensor_tensor(ang[:, 3, :], ang[:, 3, :], ang[:, 1, :], ALU.add)
            dve.drain()
            dve.tensor_scalar(ang[:, 3, :], ang[:, 3, :], -SAFE_PI, SAFE_PI, ALU.max, ALU.min)
            dve.drain().then_inc(S["setup_dve"], 1)
            for j in range(8, ADA_FIRST):
                ada_unit(0, j, ada[:, j:j + 1])
            dve.drain()
            dve.wait_ge(S["sin_ready"], 1)
            for k in range(AHEAD):
                split_lo(0, k, R0 // 4, k)
            with dve.Fori(0, DEPTH) as l:
                hb, vb, rb = l * (H1 // 4), l * (V1 // 4), R0 // 4 + l * (R1 // 4)

                def ahead(k):
                    split_lo(hb, k + AHEAD, rb, raw_of(k + AHEAD))

                centre(4 * l)
                dve.wait_ge(S["wf_hi"], l + 1)
                dve.tensor_tensor(wf_lo[:, :, :], pc("w_f").rearrange("p (c n) -> p c n", n=4),
                                  wf_hi[:, :, :].bitcast(F32), ALU.subtract).then_inc(S["wf_ready"], 1)
                dve.tensor_tensor(ada[:, 0:ADA_FIRST], ada[:, 0:ADA_FIRST], pc("b_ada")[:, 0:ADA_FIRST], ALU.add)
                dve.drain()
                dve.tensor_scalar(ada[:, 8:16], ada[:, 8:16], 1.0, None, ALU.add)
                dve.drain()
                root(4 * l)
                scale_rows(ada[:, 8:16], "ln_scaled")
                rest_u1(2 * l, ada[:, 0:8])
                for k in range(N_PROJ):
                    ahead(k)
                    if k == 1:
                        dve.wait_ge(S["f_logit"], l + 1)
                        dve.tensor_tensor(small[:, 0:8].rearrange("p (a h) -> p a h", a=2),
                                          m6[:, 0:8].rearrange("p (a h) -> p a h", a=2),
                                          pc("b_f").unsqueeze(1).broadcast_to([P, 2, 4]), ALU.add)
                        dve.drain()
                        dve.scalar_tensor_tensor(out=small[:, 8:16], in0=small[:, 0:8], scalar=-1.0, in1=small[:, 0:8],
                                                 op0=ALU.mult, op1=ALU.max).then_inc(S["f_abs"], 1)
                    if k == 3:
                        dve.wait_ge(S["f_log"], l + 1)
                        dve.scalar_tensor_tensor(out=small[:, 16:24], in0=small[:, 0:8], scalar=0.0, in1=small[:, 32:40],
                                                 op0=ALU.min, op1=ALU.subtract)
                        dve.drain()
                        dve.tensor_copy(tri_b, small[:, 16:24].unsqueeze(2).broadcast_to([P, 8, P]))\
                           .then_inc(S["logf_ready"], 1)
                    if k == 5:
                        dve.wait_ge(S["cum_ready"], l + 1)
                        dve.tensor_copy(small[:, 40:48], m6[:, 16:24])
                        dve.drain()
                        for h in range(4):
                            row = (m4, m5)[h // 2][:, (h % 2) * T:(h % 2 + 1) * T]
                            for t, (a, b) in enumerate(((0, P), (P, 3 * P))):
                                dve.scalar_tensor_tensor(out=bias[:, 4 + h, a:b], in0=row[:, 0:b - a],
                                                         scalar=small[:, 40 + 4 * t + h:41 + 4 * t + h],
                                                         in1=cc("mask")[:, a:b], op0=ALU.subtract, op1=ALU.add)
                        dve.drain().then_inc(S["bias_ready"], 1)
                    if k == 8:
                        dve.wait_ge(S["conv_in"], l + 1)
                        for c in range(2):
                            dve.tensor_tensor_scan(cs[:, c, POOL_PAD:], zeros[:, 0:T], proj[:, c, :], 0.0,
                                                   ALU.add, ALU.add)
                        dve.drain()
                    if k == 9:
                        for g, w in enumerate(POOL_WINDOWS):
                            c, b = g // 2, slice(HD * (g % 2), HD * (g % 2) + HD)
                            dve.tensor_tensor(rot_tmp[b, 2 + c, :], cs[b, c, POOL_PAD:], cs[b, c, POOL_PAD - w:POOL_PAD - w + T],
                                              ALU.subtract)
                        dve.drain()
                        dve.tensor_tensor(rot_tmp[:, 2:4, :], rot_tmp[:, 2:4, :],
                                          cc("inv_cnt").rearrange("p (a t) -> p a t", a=2), ALU.mult)
                        dve.drain()
                        dve.tensor_tensor(rot_tmp[:, 0:2, :], rot_tmp[:, 2:4, :], proj[:, 0:2, :], ALU.subtract)\
                           .then_inc(S["pooled"], 1)
                    if k == 10:
                        dve.tensor_tensor(vv[:, :, 2:], proj[:, 4:6, :], proj[:, 6:8, :], ALU.mult)
                        dve.drain()
                        for j in range(3):
                            for c in range(2):
                                w = pc("conv_w")[:, 2 * j + c:2 * j + c + 1]
                                src = vv[:, c, j:j + T]
                                if j == 0:
                                    dve.tensor_scalar(proj[:, 4 + c, :], src, w, None, ALU.mult)
                                else:
                                    dve.scalar_tensor_tensor(out=proj[:, 4 + c, :], in0=src, scalar=w, in1=proj[:, 4 + c, :],
                                                             op0=ALU.mult, op1=ALU.add)
                            dve.drain()
                        dve.tensor_tensor(proj[:, 2:4, :], proj[:, 2:4, :], proj[:, 4:6, :], ALU.mult)
                        dve.drain()
                        dve.tensor_copy(a_hi[:, 2:4, :], proj[:, 2:4, :])
                        dve.drain()
                        dve.tensor_tensor(a_lo[:, 2:4, :], proj[:, 2:4, :], a_hi[:, 2:4, :].bitcast(F32), ALU.subtract)
                    if k == 12:
                        dve.wait_ge(S["pool_mm"], l + 1)
                        for c in range(2):
                            dve.tensor_scalar(proj[:, c, :], m6[:, c * T:(c + 1) * T], pc("pool_scale")[:, c:c + 1], None,
                                              ALU.mult)
                        dve.drain()
                        dve.tensor_copy(a_hi[:, 0:2, :], proj[:, 0:2, :])
                        dve.drain()
                        dve.tensor_tensor(a_lo[:, 0:2, :], proj[:, 0:2, :], a_hi[:, 0:2, :].bitcast(F32), ALU.subtract)\
                           .then_inc(S["y_local"], 1)
                    if k == 14:
                        dve.wait_ge(S["rot_mm"], l + 1)
                        cb = cos.unsqueeze(1).broadcast_to([P, 2, T])
                        snb = sin.unsqueeze(1).broadcast_to([P, 2, T])
                        for p, bank in enumerate((m4, m5)):
                            dve.tensor_tensor(rot_tmp[:, 2 * p:2 * p + 2, :], pview(bank), snb, ALU.mult)
                            dve.tensor_tensor(rot_raw[:, 2 * p:2 * p + 2, :], rot_raw[:, 2 * p:2 * p + 2, :], cb, ALU.mult)
                        dve.drain()
                        for p in range(2):
                            dve.tensor_tensor(qk[:, 4 * p:4 * p + 2, :], rot_raw[:, 2 * p:2 * p + 2, :],
                                              rot_tmp[:, 2 * p:2 * p + 2, :], ALU.add)
                    if k >= 17 and k % 2:
                        hs, hcnt = at(hb, k)
                        c0 = (k - 17) * P
                        dve.wait_ge(mm_done[hs], hcnt + 1)
                        for t in range(2):
                            vs, _ = at(vb, k - 1 + t)
                            dve.tensor_tensor(v_tok[:, t, c0:c0 + T], ps[vs][:, 0:T], pc("b_v")[:, c0:c0 + T], ALU.add)\
                               .then_inc(psum_used[vs], 1)
                dve.wait_ge(S["proj_all"], l + 1)
                settled(dve)
                dve.drain().then_inc(S["qkv_ready"], 1)
                with dve.Fori(0, 4) as i:
                    hi_, ri_ = hb + 2 * i, rb + 4 * i
                    hc = l * 8 + 2 * i

                    def gate(k):
                        h = H1_GATE + k + AHEAD
                        ada_unit(ri_, raw_of(h) - 1, ada_t[:, k:k + 1])
                        split_lo(hi_, h, ri_, raw_of(h))

                    def negated(h):
                        dve.wait_ge(S["scores"], hc + h + 1)
                        settled(dve)
                        for t, (a, b) in enumerate(((0, P), (P, 3 * P))):
                            ins = dve.tensor_tensor_reduce(out=sneg[:, h, a:b], in0=m4[:, a:b], in1=b_st[:, h, a:b], scale=1.0,
                                                           scalar=3.0e38, op0=ALU.add, op1=ALU.min,
                                                           accum_out=mn[:, h, t:t + 1])
                        ins.then_inc(S["sneg_ready"], 1)

                    def probs(h):
                        dve.wait_ge(S["exp_done"], hc + h + 1)
                        dve.reciprocal(rs[:, h, :], rs[:, h, :])
                        dve.drain()
                        for t, (a, b) in enumerate(((0, P), (P, 3 * P))):
                            ins = dve.tensor_scalar(sneg[:, h, a:b], sneg[:, h, a:b], rs[:, h, t:t + 1], None, ALU.mult)
                        ins.then_inc(S["probs_ready"], 1)

                    gate(0)
                    dve.wait_ge(S["staged"], l * 4 + i + 1)
                    negated(0)
                    gate(1)
                    negated(1)
                    probs(0)
                    gate(2)
                    probs(1)
                    gate(3)
                    gate(4)
                    dve.wait_ge(S["o_hi_made"], l * 4 + i + 1)
                    dve.tensor_tensor(a_lo[:, 4 + i, :], m6[:, 0:T], a_hi[:, 4 + i, :].bitcast(F32), ALU.subtract)\
                       .then_inc(S["o_stored"], 1)
                    gate(5)
                    gate(6)
                    gate(7)
                    dve.drain()
                    dve.tensor_copy(ada[:, bass.ds(ADA_FIRST + 8 * i, 8)], ada_t[:, :])
                    dve.drain()
                dve.tensor_tensor(ada[:, ADA_FIRST:], ada[:, ADA_FIRST:], pc("b_ada")[:, ADA_FIRST:], ALU.add)
                dve.drain()
                dve.tensor_scalar(ada[:, 32:40], ada[:, 32:40], 1.0, None, ALU.add)
                dve.drain()
                dve.wait_ge(S["gates_ready"], l + 1)
                gates4 = gates.rearrange("p (n c) t -> p n c t", c=KC)

                def rest_merged(c):
                    dve.wait_ge(S["m_hi_made"], 8 * l + c + 1)
                    dve.scalar_tensor_tensor(out=u_lo[:, c, :], in0=msum[:, c % 2, 2, :], scalar=0.5,
                                             in1=u_hi[:, c, :].bitcast(F32), op0=ALU.mult, op1=ALU.subtract)\
                       .then_inc(S["merged"], 1)

                for c in range(KC):
                    ahead(H1_BRANCH + c)
                    hs, hcnt = at(hb, H1_BRANCH + c)
                    dve.wait_ge(mm_done[hs], hcnt + 1)
                    if c >= 2:
                        dve.wait_ge(S["msum_ready"], 8 * l + c - 1)
                    for n in range(0, 4, 2):
                        vs, _ = at(vb, V1_BRANCH + 2 * c + n // 2)
                        dve.scalar_tensor_tensor(out=prod[:, c % 2, n:n + 2, :], in0=gates4[:, n:n + 2, c, :], scalar=1.0,
                                                 in1=pview(ps[vs]), op0=ALU.add, op1=ALU.mult).then_inc(psum_used[vs], 1)
                    if c >= 2:
                        rest_merged(c - 2)
                rest_merged(KC - 2)
                rest_merged(KC - 1)
                for c in range(KC):
                    ahead(H1_WO + c)
                    hs, hcnt = at(hb, H1_WO + c)
                    vs, _ = at(vb, V1_WO + c)
                    if c == 0:
                        dve.wait_ge(S["x_scaled"], 2 * l + 1)
                    dve.wait_ge(mm_done[hs], hcnt + 1)
                    dve.scalar_tensor_tensor(out=x[:, c, :], in0=ps[vs][:, 0:T], scalar=ada[:, 16 + c:17 + c], in1=x[:, c, :],
                                             op0=ALU.mult, op1=ALU.add).then_inc(psum_used[vs], 1)
                dve.drain()
                centre(4 * l + 1)
                root(4 * l + 1)
                scale_rows(pc("ln1_g"), "x_scaled_out")
                dve.drain()
                centre(4 * l + 2)
                root(4 * l + 2)
                scale_rows(ada[:, 32:40], "ln_scaled")
                rest_u1(2 * l + 1, ada[:, 24:32])
                with dve.Fori(0, 4) as i:
                    hi_, ri_ = hb + 4 * i, rb + 5 * i
                    for k in range(16):
                        h, j = H1_FFN + k + AHEAD, k % 8
                        if k % 4 == 1:
                            ada_unit(ri_, raw_of(h) - 1, ada_t[:, k // 4:k // 4 + 1])
                        split_lo(hi_, h, ri_, raw_of(h))
                        if j < 4:
                            dve.wait_ge(S["h_hi_made"], 32 * l + 8 * i + 4 * (k // 8) + j + 1)
                            dve.tensor_tensor(a_lo[:, j, :], y[:, j, :], a_hi[:, j, :].bitcast(F32), ALU.subtract)\
                               .then_inc(S["h_ready"], 1)
                    dve.drain()
                    dve.tensor_copy(ada[:, bass.ds(4 * i, 4)], ada_t[:, 0:4])
                    dve.drain()
                dve.wait_ge(S["x_scaled"], 2 * l + 2)
                dve.wait_ge(S["ffn_done"], l + 1)
                for c in range(KC):
                    dve.scalar_tensor_tensor(out=x[:, c, :], in0=ps[4 + c // 2][:, (c % 2) * T:(c % 2 + 1) * T],
                                             scalar=ada[:, 40 + c:41 + c], in1=x[:, c, :], op0=ALU.mult, op1=ALU.add)\
                       .then_inc(S["x_chunk"], 1)
                dve.drain()
                centre(4 * l + 3)
                root(4 * l + 3)
                scale_rows(pc("ln2_g"), "x_scaled_out")

            h2_0, v2_0, r2_0 = DEPTH * (H1 // 4), DEPTH * (V1 // 4), (R0 + DEPTH * R1) // 4
            dve.wait_ge(S["table_in"], 16)
            dve.tensor_scalar(table[0:32, :], table[0:32, :], -1.0, None, ALU.mult)
            dve.memset(table[32:33, :], BIG)
            dve.drain().then_inc(S["tab_ready"], 1)
            dve.wait_ge(S["bc_mm"], 1)
            dve.tensor_copy(bc, m6[:, 0:480].rearrange("p (t n h) -> p t h n", t=2, n=CMP)).then_inc(S["bc_ready"], 1)
            for j in range(8):
                dve.wait_ge(S["flip_mm"], j + 1)
                dve.tensor_copy(bias2[:, 2 * j:2 * j + 2, :], pview((m4, m5)[j % 2])).then_inc(S["flipped"], 1)
            dve.wait_ge(S["con2_in"], 16)
            dve.drain().then_inc(S["x_ready2"], 1)

            def scaled(n, g, name):
                dve.wait_ge(S["ln_sd"], n + 1)
                dve.reciprocal(rstd[:, :], sd[:, :])
                dve.drain()
                for c in range(KC):
                    ins = dve.scalar_tensor_tensor(out=y[:, c, :], in0=x[:, c, :], scalar=g[:, c:c + 1], in1=rstd[:, :],
                                                   op0=ALU.mult, op1=ALU.mult)
                    if c % 2 and name:
                        ins.then_inc(S[name], 1)
                return ins

            with dve.Fori(0, DEPTH) as l:
                hb, vb, rb = h2_0 + l * (H2 // 4), v2_0 + l * (V2 // 4), r2_0 + l * (R2 // 4)
                n_rms = 4 * DEPTH + 2 * l
                n_u = 2 * DEPTH + 2 * l

                def ahead(k):
                    split_lo(hb, k + AHEAD, rb, k + AHEAD)

                def wait_mm(h, b=None):
                    hs, hcnt = at(hb if b is None else b, h)
                    dve.wait_ge(mm_done[hs], hcnt + 1)

                def bank_of(h, b=None):
                    return at(vb if b is None else b, h)[0]

                dve.wait_ge(S["par2_in"], 16 * (l + 1))
                scaled(n_rms, p2("g_mix"), "ln_mod")
                rest_u(n_u)
                dve.wait_ge(S["wg_hi"], l + 1)
                dve.tensor_tensor(wg_lo, p2("w_gate").rearrange("p (c n) -> p c n", n=48), wg_hi.bitcast(F32),
                                  ALU.subtract).then_inc(S["wg_ready"], 1)
                for k in range(N_KV):
                    ahead(k)
                    if k == 2:
                        dve.wait_ge(S["x2_raw"], l + 1)
                        pos = p2("pos").rearrange("p (k c) -> p k c", k=2)
                        for kind in range(2):
                            ins = dve.tensor_tensor(x2[:, kind, :, :], x2[:, kind, :, :],
                                                    pos[:, kind, :].unsqueeze(2).broadcast_to([P, CMP_LC, 2 * CMP]), ALU.add)
                        ins.then_inc(S["x2_ready"], 1)
                    if k == 4:
                        dve.wait_ge(S["x2_hi"], l + 1)
                        dve.tensor_tensor(x2_lo, x2, x2_hi.bitcast(F32), ALU.subtract).then_inc(S["x2_split"], 1)
                dve.wait_ge(S["kv_ready"], 2 * l + 2)
                dve.tensor_scalar(gsig, gsig, 0.5, 0.5, ALU.mult, ALU.add).then_inc(S["gsig_ready"], 1)
                for k in range(N_CMP):
                    ahead(H2_CMP + k)
                dve.wait_ge(S["cmp_hid"], l + 1)
                vs = bank_of(V2_HID)
                dve.tensor_copy(gx, ps[vs][0:2 * CMP, :]).then_inc(psum_used[vs], 1)
                dve.drain()
                dve.tensor_tensor(gy, gx, gx, ALU.mult)
                dve.drain()
                dve.tensor_scalar(gy, gy, GELU_CUBE, 1.0, ALU.mult, ALU.add)
                dve.drain()
                dve.tensor_tensor(gy, gy, gx, ALU.mult).then_inc(S["gelu_in"], 1)
                for k in range(KC):
                    ahead(H2_Q + k)
                    if k == 0:
                        dve.wait_ge(S["gelu_t"], l + 1)
                        dve.scalar_tensor_tensor(out=gx, in0=gz, scalar=1.0, in1=gx, op0=ALU.add, op1=ALU.mult)
                        dve.drain()
                        dve.tensor_scalar(gx, gx, 0.5, None, ALU.mult).then_inc(S["hid_ready"], 1)
                    if k == 1:
                        dve.wait_ge(S["hid_turned"], l + 1)
                        dve.tensor_copy(hx, m6[:, 256:376]).then_inc(S["hx_ready"], 1)
                    if k == 2:
                        dve.wait_ge(S["cmp_w2"], l + 1)
                        dve.tensor_copy(kct, m5[:, 0:30])
                        dve.tensor_copy(vcn, m5[0:CMP, 64:192])
                        dve.drain().then_inc(S["cmp_kv"], 1)
                    if k == 4:
                        dve.wait_ge(S["vrep"], l + 1)
                        for g in range(2):
                            ins = dve.tensor_tensor(vbd[:, g, :, :], m6[:, HD * g:HD * (g + 1)].unsqueeze(1)
                                                    .broadcast_to([P, 8, HD]),
                                                    c2("blocks").rearrange("p (h d) -> p h d", h=8), ALU.mult)
                        ins.then_inc(S["vbd_ready"], 1)
                dve.wait_ge(S["cmp_sc"], l + 1)
                for t in range(2):
                    for j in range(2):
                        dve.tensor_tensor(sc_cmp[:, t, j::2, :],
                                          (m4, m5)[j][:, 120 * t:120 * t + 120].rearrange("p (h n) -> p h n", h=8),
                                          bc[:, t, j::2, :], ALU.add)
                dve.memset(pc_n, 0.0)
                dve.drain()
                sc3 = sc_cmp.rearrange("p t h n -> p (t h) n")
                dve.tensor_reduce(st_c[:, 0, :], sc3, AX.X, ALU.min)
                dve.drain()
                dve.tensor_tensor(sc3, sc3, st_c[:, 0, :].unsqueeze(2).broadcast_to([P, 32, CMP]), ALU.subtract)\
                   .then_inc(S["cmp_neg"], 1)

                def cmp_probs():
                    dve.wait_ge(S["cmp_exp"], l + 1)
                    mask = c2("cmask").rearrange("p (t n) -> p t n", t=2)
                    for t in range(2):
                        dve.tensor_tensor(sc_cmp[:, t, :, :], sc_cmp[:, t, :, :],
                                          mask[:, t, :].unsqueeze(1).broadcast_to([P, NSA_HEADS, CMP]), ALU.mult)
                    dve.drain()
                    dve.tensor_reduce(st_c[:, 1, :], sc3, AX.X, ALU.add)
                    dve.drain()
                    dve.tensor_scalar(st_c[:, 1, :], st_c[:, 1, :], 1e-30, None, ALU.max)
                    dve.drain()
                    dve.reciprocal(st_c[:, 2, :], st_c[:, 1, :])
                    dve.drain()
                    dve.tensor_tensor(st_c[:, 2, :].rearrange("p (t h) -> p t h", t=2),
                                      st_c[:, 2, :].rearrange("p (t h) -> p t h", t=2), gsig[:, :, :, 0], ALU.mult)
                    dve.drain()
                    for t in range(2):
                        ins = dve.tensor_tensor(pc_n[:, t, :, 0:CMP], sc_cmp[:, t, :, :],
                                                st_c[:, 2, 16 * t:16 * t + 16].unsqueeze(2)
                                                .broadcast_to([P, NSA_HEADS, CMP]), ALU.mult)
                    ins.then_inc(S["cmp_p"], 1)

                cmp_probs()
                for g in range(NSA_GROUPS):
                    with dve.Fori(0, 4) as i:
                        hi_, ri_ = hb + i, rb + i
                        hc = l * NSA_HEADS + 8 * g + 2 * i

                        def unit(k):
                            h = (H2_QK, H2_V)[g] + k + AHEAD
                            split_lo(hi_, h, ri_, h)

                        def negated(h):
                            dve.wait_ge(S["n_scores"], hc + h + 1)
                            settled(dve)
                            for kind in range(2):
                                j = 2 * h + kind
                                dve.tensor_tensor_reduce(out=sn[:, j, 0:P], in0=m5[:, kind * P:(kind + 1) * P],
                                                         in1=b_st2[:, h, P:T], scale=1.0, scalar=3.0e38, op0=ALU.add,
                                                         op1=ALU.min, accum_out=mn2[:, j, 0:1])
                                dve.tensor_tensor_reduce(out=sn[:, j, P:384], in0=m4[:, kind * T:(kind + 1) * T],
                                                         in1=b_st2[:, h, :], scale=1.0, scalar=3.0e38, op0=ALU.add,
                                                         op1=ALU.min, accum_out=mn2[:, j, 1:2]).then_inc(S["n_sneg"], 1)

                        def probs(h):
                            for kind in range(2):
                                j = 2 * h + kind
                                dve.wait_ge(S["n_exp"], 2 * (hc + h) + kind + 1)
                                dve.reciprocal(w_st[:, h, kind, :], rs2[:, j, :])
                                dve.drain()
                                dve.tensor_tensor(w_st[:, h, kind, :], w_st[:, h, kind, :],
                                                  gsig[:, :, 8 * g + 2 * i + h, 2 - kind], ALU.mult)
                                dve.drain()
                                dve.tensor_scalar(sn[:, j, 0:P], sn[:, j, 0:P], w_st[:, h, kind, 0:1], None, ALU.mult)
                                dve.tensor_scalar(sn[:, j, P:384], sn[:, j, P:384], w_st[:, h, kind, 1:2], None, ALU.mult)\
                                   .then_inc(S["n_probs"], 1)

                        dve.wait_ge(S["staged2"], 8 * l + 4 * g + i + 1)
                        negated(0)
                        unit(0)
                        probs(0)
                        negated(1)
                        unit(1)
                        probs(1)
                        unit(2)
                        unit(3)
                        if g == 1:
                            dve.wait_ge(S["v_ready"], 4 * l + i + 1)
                            dve.tensor_reduce(vm[:, :], rv[:, i, :, :], AX.X, ALU.add)
                            dve.drain()
                            dve.tensor_scalar(vm[:, :], vm[:, :], -1.0 / RET_DV, None, ALU.mult)
                            dve.drain()
                            for t in range(2):
                                ins = dve.tensor_scalar(rv[:, i, t, :], rv[:, i, t, :], vm[:, t:t + 1], None, ALU.add)
                            ins.then_inc(S["v_cent"], 1)
                dve.wait_ge(S["cmp_o"], l + 1)
                for p in range(4):
                    ins = dve.tensor_tensor(y[:, 2 * p:2 * p + 2, :], pview(ps[4 + p]), y[:, 2 * p:2 * p + 2, :], ALU.add)
                ins.then_inc(S["cmp_stored"], 1)
                decay = c2("decay").rearrange("p (h t) -> p h t", h=RET_HEADS)
                for p in range(2):
                    h0 = H2_PAIR + 16 * p
                    nh = 4 * l + 2 * p
                    ny = 16 * l + 8 * p

                    def decayed(j):
                        dve.wait_ge(S["r_st"], nh + j + 1)
                        bank, d = (m4, m5)[j], decay[:, 2 * p + j, :]
                        dve.tensor_tensor(sn[:, j, 0:T], bank[:, 0:T], d, ALU.mult)
                        dve.tensor_tensor(sn[:, j, T:384], bank[:, T:384], d[:, 0:P], ALU.mult).then_inc(S["r_sts"], 1)

                    def taken(j):
                        dve.wait_ge(S["r_ot"], nh + j + 1)
                        o = rv[:, 2 * p + j, :, :].rearrange("p a (b t) -> p (a b) t", t=T)
                        for m in range(2):
                            ins = dve.tensor_copy(o[:, 2 * m:2 * m + 2, :], pview(((m6, m7), (m4, m5))[j][m]))
                        ins.then_inc(S["r_copy"], 1)

                    def normed(j):
                        dve.wait_ge(S["r_sd"], nh + j + 1)
                        dve.reciprocal(rstd[:, :], (sd[:, :], rt[:, 0, :])[j])
                        dve.drain()
                        o = rv[:, 2 * p + j, :, :].rearrange("p a (b t) -> p (a b) t", t=T)
                        for m in range(2):
                            ins = dve.tensor_tensor(o[:, 2 * m:2 * m + 2, :], o[:, 2 * m:2 * m + 2, :],
                                                    rstd[:, :].unsqueeze(1).broadcast_to([P, 2, T]), ALU.mult)
                        dve.drain()
                        dve.nop().then_inc(S["r_norm"], 1)

                    def rest_y(c):
                        dve.wait_ge(S["y_hi"], ny + c + 1)
                        dve.tensor_tensor(a_lo[:, c, :], pt2[:, c % 2, 0:T], a_hi[:, c, :].bitcast(F32), ALU.subtract)\
                           .then_inc(S["y_full"], 1)

                    decayed(0)
                    decayed(1)
                    for k in range(8):
                        ahead(h0 + k)
                        if k == 1:
                            taken(0)
                        if k == 3:
                            taken(1)
                        dve.wait_ge(S["g2_tanh"], ny + k + 1)
                        v = bank_of(h0 + k + V2_SHIFT)
                        dve.scalar_tensor_tensor(out=sg[:, k, :], in0=tmpa[:, k % 2, :], scalar=1.0, in1=ps[v][:, 0:T],
                                                 op0=ALU.add, op1=ALU.mult).then_inc(psum_used[v], 1)
                        dve.drain().then_inc(S["sg_ready"], 1)
                        if k == 4:
                            normed(0)
                        if k == 5:
                            normed(1)
                    rest_y(0)
                    rest_y(1)
                    ahead(h0 + 8)
                    rest_y(2)
                    rest_y(3)
                    ahead(h0 + 9)
                    for c in range(4, KC):
                        rest_y(c)
                    for c in range(KC):
                        if c >= 2:
                            ahead(h0 + 8 + c)
                        if p == 1 and c >= 1:
                            wait_mm(h0 + 8 + c - 1)
                            v = bank_of(h0 + 8 + c - 1 + V2_SHIFT)
                            dve.tensor_tensor(yret[:, c - 1, :], ps[v][:, 0:T], yret[:, c - 1, :], ALU.add)\
                               .then_inc(psum_used[v], 1)
                    if p == 1:
                        wait_mm(h0 + 15)
                        v = bank_of(h0 + 15 + V2_SHIFT)
                        dve.tensor_tensor(yret[:, 7, :], ps[v][:, 0:T], yret[:, 7, :], ALU.add).then_inc(psum_used[v], 1)
                        dve.drain()
                for k in range(2 * KC):
                    ahead(H2_MA + k)
                    if k < KC:
                        vs, vc = at(vb, H2_MA + k + V2_SHIFT)
                        dve.wait_ge(psum_used[vs], vc + 1)
                        dve.scalar_tensor_tensor(out=yret[:, k, :], in0=tmpa[:, k % 2, :], scalar=1.0, in1=yret[:, k, :],
                                                 op0=ALU.add, op1=ALU.mult).then_inc(S["ma_all"], 1)
                        if k % 2:
                            pr = k // 2
                            dve.wait_ge(S["nsa_hi"], 4 * l + pr + 1)
                            dve.tensor_tensor(a_lo[:, 2 * pr:2 * pr + 2, :], y[:, 2 * pr:2 * pr + 2, :],
                                              a_hi[:, 2 * pr:2 * pr + 2, :].bitcast(F32), ALU.subtract)\
                               .then_inc(S["nsa_full"], 1)
                nm = 8 * DEPTH + 8 * l

                def rest_merged(c):
                    dve.wait_ge(S["m_hi_made"], nm + c + 1)
                    dve.scalar_tensor_tensor(out=u_lo[:, c, :], in0=pt2[:, c % 2, 0:T], scalar=0.5,
                                             in1=u_hi[:, c, :].bitcast(F32), op0=ALU.mult, op1=ALU.subtract)\
                       .then_inc(S["merged"], 1)

                dve.wait_ge(S["mb_all"], l + 1)
                for c in range(KC):
                    ahead(H2_ONSA + c)
                    wait_mm(H2_ONSA + c)
                    v = bank_of(H2_ONSA + c + V2_SHIFT)
                    dve.scalar_tensor_tensor(out=tmpa[:, c % 2, :], in0=sig_b[:, c, :], scalar=1.0, in1=ps[v][:, 0:T],
                                             op0=ALU.add, op1=ALU.mult).then_inc(psum_used[v], 1)
                    if c >= 2:
                        rest_merged(c - 2)
                    dve.drain()
                    dve.tensor_tensor(pt2[:, c % 2, 0:T], tmpa[:, c % 2, :], yret[:, c, :], ALU.add)\
                       .then_inc(S["msum_ready"], 1)
                rest_merged(KC - 2)
                rest_merged(KC - 1)
                for c in range(KC):
                    ahead(H2_OUT + c)
                    wait_mm(H2_OUT + c)
                    v = bank_of(H2_OUT + c + V2_SHIFT)
                    dve.tensor_tensor(x[:, c, :], ps[v][:, 0:T], x[:, c, :], ALU.add).then_inc(psum_used[v], 1)
                dve.drain()
                scaled(n_rms + 1, p2("g_ffn"), "ln_mod")
                rest_u(n_u + 1)

                def ffn(hx_, vx_, rx_, h0, v0, order, n0):
                    v, late = v0, None

                    def rest_hidden(k):
                        dve.wait_ge(S["h_hi_made"], n0 + k + 1)
                        dve.tensor_tensor(a_lo[:, k, :], y[:, k, :], a_hi[:, k, :].bitcast(F32), ALU.subtract)\
                           .then_inc(S["h_ready"], 1)

                    for idx, (what, k) in enumerate(order):
                        h = h0 + idx
                        split_lo(hx_, h + AHEAD, rx_, h + AHEAD)
                        if late is not None:
                            rest_hidden(late)
                            late = None
                        if what == "b":
                            va, vbk = at(vx_, v - 1)[0], at(vx_, v)[0]
                            dve.wait_ge(S["t2_made"], n0 - 32 * DEPTH + k + 1)
                            dve.scalar_tensor_tensor(out=tmpa[:, k % 2, :], in0=pt2[:, k % 2, 0:T], scalar=1.0,
                                                     in1=ps[va][:, 0:T], op0=ALU.add, op1=ALU.mult)\
                               .then_inc(psum_used[va], 1)
                            dve.drain()
                            hs, hcnt = at(hx_, h)
                            dve.wait_ge(mm_done[hs], hcnt + 1)
                            dve.scalar_tensor_tensor(out=y[:, k, :], in0=tmpa[:, k % 2, :], scalar=0.5,
                                                     in1=ps[vbk][:, 0:T], op0=ALU.mult, op1=ALU.mult)\
                               .then_inc(psum_used[vbk], 1)
                            late = k
                        if what != "d":
                            v += 1
                    if late is not None:
                        rest_hidden(late)

                n_h = 32 * DEPTH + FFN2 * l
                with dve.Fori(0, 5) as i:
                    ffn(hb + 3 * i, vb + 2 * i, rb + 3 * i, H2_FFN, V2_FFN, BODY2, n_h + 4 * i)
                ffn(hb, vb, rb, H2_FFN + 60, V2_FFN + 40, TAIL2, n_h + 20)
                dve.wait_ge(S["ffn_done"], DEPTH + l + 1)
                for c in range(4):
                    dve.tensor_tensor(x[:, 2 * c:2 * c + 2, :], pview(ps[4 + c]), x[:, 2 * c:2 * c + 2, :], ALU.add)
                dve.drain().then_inc(S["x_ready2"], 1)
            scaled(6 * DEPTH, c2("g_final"), None).then_inc(S["y_last"], 1)

        @block.gpsimd
        def _(pool):
            with pool.Fori(0, DEPTH) as l:
                pool.wait_ge(S["ln_cent"], 16 * l + 4)
                settled(pool)
                pool.tensor_scalar(x[:, :, :], x[:, :, :], ALPHA, None, ALU.mult).then_inc(S["x_scaled"], 1)
                pool.wait_ge(S["qkv_ready"], l + 1)
                settled(pool)
                with pool.Fori(0, 4) as i:
                    pool.wait_ge(S["pv_done"], l * 8 + 2 * i)
                    pool.tensor_copy(q_st, qk[:, i, :])
                    pool.tensor_copy(k_st, qk[:, 4 + i, :])
                    pool.tensor_copy(b_st, bias[:, bass.ds(2 * i, 2), :])
                    pool.tensor_copy(v_st, v_tok[:, :, bass.ds(P * i, P)])
                    pool.drain().then_inc(S["staged"], 1)
                for c in range(KC):
                    pool.wait_ge(psum_used[(V1_BRANCH + 2 * c + 1) % RING], l * (V1 // 4) + (V1_BRANCH + 2 * c + 1) // RING + 1)
                    if c >= 2:
                        pool.wait_ge(S["merged"], 8 * l + c - 1)
                    for n in range(2):
                        pool.tensor_tensor(msum[:, c % 2, n, :], prod[:, c % 2, 2 * n, :], prod[:, c % 2, 2 * n + 1, :], ALU.add)
                    pool.drain()
                    pool.tensor_tensor(msum[:, c % 2, 2, :], msum[:, c % 2, 0, :], msum[:, c % 2, 1, :], ALU.add)\
                        .then_inc(S["msum_ready"], 1)
                pool.wait_ge(S["ln_cent"], 16 * l + 12)
                settled(pool)
                pool.tensor_scalar(x[:, :, :], x[:, :, :], ALPHA, None, ALU.mult).then_inc(S["x_scaled"], 1)


            pool.wait_ge(S["layer_end"], DEPTH)
            pool.wait_ge(S["con2_in"], 16)
            pool.nop().then_inc(S["rr_done"], 1)

            def stage(l, c):
                pool.wait_ge(S["n_sneg"], 4 * (8 * l + c))
                settled(pool)
                pool.tensor_copy(q_st2, qn[:, c, :])
                pool.tensor_copy(b_st2, bias2[:, bass.ds(2 * c, 2), :])
                pool.drain().then_inc(S["staged2"], 1)

            def rotate(dst, c, j):
                x1, x2_ = r4[:, j, :], r4[:, j + 1, :]
                pool.tensor_tensor(rt[:, 0, :], x1, c2("cos"), ALU.mult)
                pool.tensor_tensor(rt[:, 1, :], x2_, c2("sin"), ALU.mult)
                pool.drain()
                pool.tensor_tensor(dst[:, 2 * c, :], rt[:, 0, :], rt[:, 1, :], ALU.subtract)
                pool.drain()
                pool.tensor_tensor(rt[:, 0, :], x1, c2("sin"), ALU.mult)
                pool.tensor_tensor(rt[:, 1, :], x2_, c2("cos"), ALU.mult)
                pool.drain()
                pool.tensor_tensor(dst[:, 2 * c + 1, :], rt[:, 0, :], rt[:, 1, :], ALU.add)
                pool.drain().then_inc(S["rr_done"], 1)

            with pool.Fori(0, DEPTH) as l:
                pool.wait_ge(S["q_all"], l + 1)
                pool.wait_ge(S["flipped"], 8)
                settled(pool)
                stage(l, 0)
                with pool.Fori(0, 4) as i:
                    pool.wait_ge(S["rr_ready"], 8 * l + 2 * i + 1)
                    rotate(rq, i, 0)
                    stage(l, i + 1)
                    pool.wait_ge(S["rr_ready"], 8 * l + 2 * i + 2)
                    rotate(rk, i, 2)
                with pool.Fori(0, 3) as i:
                    stage(l, i + 5)
                for p in range(2):
                    for c in range(KC):
                        if c % 4 == 0:
                            pool.wait_ge(S["r_norm"], 4 * l + 2 * p + c // 4 + 1)
                        pool.wait_ge(S["sg_ready"], 16 * l + 8 * p + c + 1)
                        if c >= 2:
                            pool.wait_ge(S["y_full"], 16 * l + 8 * p + c - 1)
                        o = rv[:, 2 * p + c // 4, :, :].rearrange("p a (b t) -> p (a b) t", t=T)
                        pool.tensor_tensor(pt2[:, c % 2, 0:T], sg[:, c, :], o[:, c % 4, :], ALU.mult)\
                            .then_inc(S["y_ready"], 1)


def chunked(v):
    return np.ascontiguousarray(v.reshape(-1, P).T)


def k_units(w):
    r, c = w.shape
    a = w.reshape(r // D, KC, P, c // P, P)
    return a.transpose(3, 0, 2, 1, 4).reshape(-1, P, UW)


def first_stream(w_ada, w_next, w_in, w_branch, w_o, w_up, w_down):
    wi = np.concatenate([w_in[:, 0:1536], w_in[:, 1792:2304], w_in[:, 1536:1792], w_in[:, 2304:2560]], axis=1)
    pr = k_units(wi)
    gate = k_units(w_in[:, 2564:])
    ad = w_ada.reshape(D, ADA, P).transpose(1, 2, 0)
    nx = w_next.reshape(D, ADA, P).transpose(1, 2, 0)
    br = k_units(w_branch.reshape(D, D))
    wo = k_units(w_o)
    up = k_units(w_up)
    down = w_down.reshape(32, P, D)
    units = [pr, gate, br, wo]
    for i in range(8):
        units += [up[4 * i:4 * i + 4], down[4 * i:4 * i + 4]]
    units = np.concatenate(units)
    out = np.empty((R1 + AHEAD, P, UW), np.float32)
    where = [raw_of(h) for h in range(H1)]
    out[where] = units
    rest = [r for r in range(R1) if r not in where]
    out[rest] = np.concatenate([ad[ADA_FIRST:], nx[0:ADA_FIRST]])
    return out[0:R1]


def constants1():
    rot = np.zeros((P, P), np.float32)
    inv = np.zeros((P, 1), np.float32)
    f = (np.float32(500000.0) ** (-np.arange(0, 16, 2, dtype=np.float32) / np.float32(16))).astype(np.float32)
    for h in range(2):
        for j in range(8):
            a, b = HD * h + j, HD * h + 8 + j
            rot[b, a] = -1.0
            rot[a, b] = 1.0
            inv[a] = inv[b] = f[j]
    t = np.arange(T)
    tri = np.stack([(kt * P + np.arange(P))[:, None] <= t[None] for kt in range(2)], 1).astype(np.float32)
    q = np.arange(P)[:, None]
    mask = np.concatenate([np.where(np.arange(P)[None] > q, BIG, 0), np.where(t[None] > q + P, BIG, 0)], 1)
    cnt = np.stack([1.0 / np.minimum(t + 1, w).astype(np.float32) for w in POOL_WINDOWS])
    inv_cnt = np.stack([np.repeat(cnt[2 * c:2 * c + 2], HD, 0) for c in range(2)], 1)
    return np.concatenate([rot, inv, tri.reshape(P, -1), mask, inv_cnt.reshape(P, -1)], 1).astype(np.float32)


def params1(b_ada, b_in, b_up, ln1_g, ln1_b, ln2_g, ln2_b, pool_scale, conv_w, w_in, w_pool):
    bp = np.concatenate([b_in[0:1536], b_in[1792:2304]])
    bv = np.concatenate([b_in[1536:1792], b_in[2304:2560]])
    wp = np.zeros((P, 2, P), np.float32)
    for g in range(4):
        o = HD * (g % 2)
        wp[o:o + HD, g // 2, o:o + HD] = w_pool[g]
    cw = conv_w.reshape(3, 2, P).transpose(2, 0, 1).reshape(P, 6)
    wf = w_in[:, 2560:2564].reshape(KC, P, 4).transpose(1, 0, 2).reshape(P, 32)
    return np.concatenate([chunked(b_ada), chunked(bp), chunked(b_in[2564:]), chunked(b_up), chunked(ln1_g), chunked(ln1_b),
                           chunked(ln2_g), chunked(ln2_b), chunked(pool_scale), cw, np.broadcast_to(bv, (P, 512)),
                           np.broadcast_to(b_in[2560:2564], (P, 4)), wf, wp.reshape(P, 256)], 1)


def second_stream(w_in, w1_k, w1_v, w_o_ret, w_o_nsa, w_out, w_ffn_in, w_ffn_out):
    rq, rk, rv = (k_units(w_in[:, a:b]) for a, b in ((0, 1024), (1024, 2048), (2048, 4096)))
    gate = k_units(w_in[:, 4096:6144])
    qn = k_units(w_in[:, 6144:7168])
    kv = k_units(w_in[:, 7168:7936])[[0, 1, 2, 4, 5, 3]]
    ma, mb = k_units(w_in[:, 7984:9008]), k_units(w_in[:, 9008:10032])
    cmp = [w.reshape(4, 4, P, 256).transpose(0, 2, 1, 3).reshape(4, P, UW) for w in (w1_k, w1_v)]
    parts = [kv, *cmp, qn]
    for i in range(4):
        parts += [rq[2 * i:2 * i + 2], rk[2 * i:2 * i + 2]]
    parts.append(rv)
    for p in range(2):
        parts += [gate[8 * p:8 * p + 8], k_units(w_o_ret[D * p:D * (p + 1)])]
    parts += [ma, mb, k_units(w_o_nsa), k_units(w_out)]
    f = FFN2 * P
    src = {"a": k_units(w_ffn_in[:, 0:f]), "b": k_units(w_ffn_in[:, f:]), "d": w_ffn_out.reshape(FFN2, P, D)}
    for i in range(5):
        parts += [src[what][4 * i + k][None] for what, k in BODY2]
    parts += [src[what][20 + k][None] for what, k in TAIL2]
    return np.concatenate(parts)


def bucket(dist):
    dist = np.maximum(dist, 0)
    large = 16 + (np.log(np.maximum(dist, 1).astype(np.float32) / np.float32(16)) / np.float32(math.log(8.0))
                  * np.float32(16)).astype(np.int32)
    return np.where(dist < 16, dist, np.minimum(large, 31))


def one_hot_distances():
    d = 255 - np.arange(HOT_ROW)
    dc = (np.arange(T).reshape(2, 1, P) - (CMP_STRIDE * np.arange(CMP) + 31)[None, :, None]).reshape(-1)
    both = np.concatenate([d, dc])
    out = np.zeros((HOT, both.size), np.float32)
    out[np.where(both < 0, 32, bucket(both)), np.arange(both.size)] = 1.0
    return out


def constants2(g_final):
    f = (np.float32(10000.0) ** (-np.arange(P, dtype=np.float32) / np.float32(P))).astype(np.float32)
    a = (np.arange(T, dtype=np.float32)[None] * f[:, None]).astype(np.float32)
    lg = np.log(1.0 - 2.0 ** (-5.0 - np.arange(RET_HEADS)))
    n, m = np.arange(T)[None, None], np.arange(P)[:, None, None]
    decay = np.where(n >= m, np.exp(np.maximum(n - m, 0) * lg[None, :, None]), 0.0) / 16.0
    pos = np.arange(P)[:, None, None] + P * np.arange(2)[None, :, None]
    cmask = (pos >= (CMP_STRIDE * np.arange(CMP) + 31)[None, None]).astype(np.float32)
    blocks = np.repeat(np.arange(P)[:, None] // 16 == np.arange(8)[None], HD, axis=1)
    rep = np.zeros((P, P), np.float32)
    for h in range(8):
        for j in range(CMP):
            rep[j, 16 * h + j] = 1.0
    return np.concatenate([np.cos(a), np.sin(a), decay.reshape(P, -1), cmask.reshape(P, -1), blocks, rep,
                           chunked(g_final)], 1).astype(np.float32)


def params2(g_mix, g_ffn, w_in, pos_k, pos_v, w2_k, w2_v):
    wg = w_in[:, 7936:7984].reshape(KC, P, 48).transpose(1, 0, 2).reshape(P, 384)
    pos = [p.reshape(CMP_LC, P).T for p in (pos_k, pos_v)]
    k2 = w2_k.reshape(2, P, HD).transpose(1, 0, 2)
    k2 = np.concatenate([k2, k2], axis=2).reshape(P, 256)
    v2 = w2_v.reshape(2, P, HD).transpose(1, 0, 2).reshape(P, 128)
    return np.concatenate([chunked(g_mix), chunked(g_ffn), wg, *pos, k2, v2], 1)


def kernel(x, c, positions, w_ada, b_ada, w_in, b_in, w_pool, pool_scale, conv_w, w_branch, w_o, ln1_g, ln1_b, w_up, b_up,
           w_down, ln2_g, ln2_b, norm_mix_g_2, w_in_2, cmp_pos_k_2, cmp_pos_v_2, cmp_w1_k_2, cmp_w2_k_2, cmp_w1_v_2,
           cmp_w2_v_2, w_o_ret_2, w_o_nsa_2, w_out_2, norm_ffn_g_2, w_ffn_in_2, w_ffn_out_2, rel_bias_2, norm_final_g_2):
    import concourse.bacc as bacc
    from concourse.bass_utils import run_bass_kernel_spmd

    stream = [w_ada[0].reshape(D, ADA, P).transpose(1, 2, 0)[0:ADA_FIRST]]
    stream += [first_stream(w_ada[l], w_ada[min(l + 1, DEPTH - 1)], w_in[l], w_branch[l], w_o[l], w_up[l], w_down[l]) for l in range(DEPTH)]
    stream += [second_stream(w_in_2[l], cmp_w1_k_2[l], cmp_w1_v_2[l], w_o_ret_2[l], w_o_nsa_2[l], w_out_2[l], w_ffn_in_2[l],
                             w_ffn_out_2[l]) for l in range(DEPTH)]
    stream.append(np.zeros((RING, P, UW), np.float32))
    arrays = {
        "stream": np.concatenate(stream).reshape(-1, RING, P, UW),
        "x_in": x[0].T.reshape(KC, P, T).transpose(1, 0, 2),
        "c_in": c[0],
        "positions": positions.reshape(T),
        "par1": np.stack([params1(b_ada[l], b_in[l], b_up[l], ln1_g[l], ln1_b[l], ln2_g[l], ln2_b[l], pool_scale[l],
                                  conv_w[l], w_in[l], w_pool[l]) for l in range(DEPTH)]),
        "con1": constants1(),
        "ident_in": np.eye(P, dtype=np.float32),
        "par2": np.stack([params2(norm_mix_g_2[l], norm_ffn_g_2[l], w_in_2[l], cmp_pos_k_2[l], cmp_pos_v_2[l],
                                  cmp_w2_k_2[l], cmp_w2_v_2[l]) for l in range(DEPTH)]),
        "con2": constants2(norm_final_g_2),
        "flip_in": np.eye(P, dtype=np.float32)[::-1],
        "hot": one_hot_distances(),
        "rel_bias": rel_bias_2,
    }
    arrays = {k: np.ascontiguousarray(v) for k, v in arrays.items()}
    nc = bacc.Bacc("TRN2", target_bir_lowering=False, num_devices=1)
    args = {k: nc.dram_tensor(k, v.shape, mybir.dt.from_np(v.dtype), kind="ExternalInput").ap() for k, v in arrays.items()}
    args["fn_dram"] = nc.dram_tensor("fn_dram", (NSA_HEADS, HOT_ROW), F32, kind="Internal").ap()
    args["out"] = nc.dram_tensor("out", (P, KC, T), F32, kind="ExternalOutput").ap()
    build_program(nc, **args)
    r = run_bass_kernel_spmd(nc, [arrays], core_ids=[0])
    return r.results[0]["out"].transpose(1, 0, 2).reshape(D, T).T.reshape(1, T, D)
```
